# Optimizing a Trainium2 kernel written in Bass

```python
import jax, jax.numpy as jnp
from jax import lax
import numpy as np

D_MODEL = 1024
BATCH = 1
SEQ = 512
DEPTH = 1

CHUNK = 64
ROPE_THETA = 10000.0
EPS = 1e-6

RET_HEADS = 4
RET_DK = 64
RET_DV = 128
SWA_Q_HEADS = 8
SWA_KV_HEADS = 2
SWA_HD = 64
SWA_WINDOW = 128
SWA_WINDOW_CHUNKS = SWA_WINDOW // CHUNK
HG_HEADS = 4
HG_DK = 128
HG_DV = 128
HG_BLOCK = 16
MEM_LEN = 256
MEM_HEADS = 4
MEM_HD = 128
D_FF = 2816
CONV_W = 3

N_BRANCH = 3
BRANCH_W = 512
IN_SIZES = (RET_HEADS * RET_DK, RET_HEADS * RET_DK, RET_HEADS * RET_DV, RET_HEADS * RET_DV,
            SWA_Q_HEADS * SWA_HD, SWA_KV_HEADS * SWA_HD, SWA_KV_HEADS * SWA_HD,
            HG_HEADS * HG_DK, HG_HEADS * HG_DK, HG_HEADS * HG_DV, HG_HEADS * HG_DV,
            N_BRANCH * D_MODEL)
IN_COLS = sum(IN_SIZES)

kernel_name = "hybrid_ret_swa_hgrn2_block"

def rms_norm(x, g):
    xf = x.astype(jnp.float32)
    y = xf * lax.rsqrt(jnp.mean(xf * xf, axis=-1, keepdims=True) + EPS)
    return (y * g.astype(jnp.float32)).astype(x.dtype)

def head_rms(y):
    yf = y.astype(jnp.float32)
    return (yf * lax.rsqrt(jnp.mean(yf * yf, axis=-1, keepdims=True) + EPS)).astype(y.dtype)

def rope_tables(positions, dim):
    inv = 1.0 / (ROPE_THETA ** (jnp.arange(0, dim, 2, dtype=jnp.float32) / dim))
    ang = positions.astype(jnp.float32)[..., None] * inv
    return jnp.cos(ang), jnp.sin(ang)

def apply_rope(t, cos, sin):
    c = cos[:, :, None, :].astype(t.dtype)
    s = sin[:, :, None, :].astype(t.dtype)
    t1, t2 = jnp.split(t, 2, axis=-1)
    return jnp.concatenate([t1 * c - t2 * s, t2 * c + t1 * s], axis=-1)

def retention(q, k, v, g, cos, sin):
    B, S, H, dk = q.shape
    dv = v.shape[-1]
    L = CHUNK
    nC = S // L
    dt = q.dtype
    q = apply_rope(q, cos, sin)
    k = apply_rope(k, cos, sin) * (dk ** -0.5)
    log_gamma = jnp.log1p(-jnp.exp2(-5.0 - jnp.arange(H, dtype=jnp.float32)))
    idx = jnp.arange(L, dtype=jnp.float32)
    diff = idx[:, None] - idx[None, :]
    decay_in = jnp.where(diff[None] >= 0,
                         jnp.exp(log_gamma[:, None, None] * jnp.maximum(diff, 0.0)[None]), 0.0).astype(dt)
    q_decay = jnp.exp((idx + 1.0)[:, None] * log_gamma[None]).astype(dt)
    k_decay = jnp.exp((L - 1.0 - idx)[:, None] * log_gamma[None]).astype(dt)
    chunk_decay = jnp.exp(L * log_gamma).astype(dt)
    qc = q.reshape(B, nC, L, H, dk)
    kc = k.reshape(B, nC, L, H, dk)
    vc = v.reshape(B, nC, L, H, dv)
    scores = jnp.einsum('bcnhd,bcmhd->bchnm', qc, kc) * decay_in[None, None]
    inner = jnp.einsum('bchnm,bcmhe->bcnhe', scores, vc)
    upd = jnp.einsum('bcmhd,bcmhe->bchde', kc * k_decay[None, None, :, :, None], vc)

    def step(R, u):
        return R * chunk_decay[None, :, None, None] + u, R

    _, R_prev = lax.scan(step, jnp.zeros_like(upd[:, 0]), jnp.moveaxis(upd, 1, 0))
    cross = jnp.einsum('bcnhd,cbhde->bcnhe', qc * q_decay[None, None, :, :, None], R_prev)
    y = (inner + cross).reshape(B, S, H, dv)
    y = head_rms(y) * jax.nn.silu(g)
    return y.reshape(B, S, H * dv)

def _band(t):
    nprev = SWA_WINDOW_CHUNKS - 1
    nC = t.shape[1]
    tp = jnp.pad(t, ((0, 0), (nprev, 0), (0, 0), (0, 0), (0, 0)))
    return jnp.concatenate([tp[:, j:j + nC] for j in range(SWA_WINDOW_CHUNKS)], axis=2)

def swa_with_sinks(q, k, v, sinks, cos, sin):
    B, S, Hq, hd = q.shape
    Hkv = k.shape[2]
    G = Hq // Hkv
    L = CHUNK
    nC = S // L
    q = apply_rope(q, cos, sin) * (hd ** -0.5)
    k = apply_rope(k, cos, sin)
    qc = q.reshape(B, nC, L, Hkv, G, hd)
    kb = _band(k.reshape(B, nC, L, Hkv, hd))
    vb = _band(v.reshape(B, nC, L, Hkv, hd))
    s = jnp.einsum('bcqhgd,bckhd->bchgqk', qc, kb).astype(jnp.float32)
    slot_chunk = jnp.arange(SWA_WINDOW_CHUNKS * L) // L
    valid = (jnp.arange(nC)[:, None] + slot_chunk[None, :]) >= (SWA_WINDOW_CHUNKS - 1)
    s = jnp.where(valid[None, :, None, None, None, :], s, -1e30)
    sink = jnp.broadcast_to(sinks.astype(jnp.float32).reshape(Hkv, G)[None, None, :, :, None, None],
                            s.shape[:-1] + (1,))
    p = jax.nn.softmax(jnp.concatenate([s, sink], axis=-1), axis=-1)[..., :-1].astype(v.dtype)
    o = jnp.einsum('bchgqk,bckhd->bcqhgd', p, vb)
    return o.reshape(B, S, Hq * hd)

def hgrn2(q, f, i, og, lb, norm_g):
    B, S, H, dk = q.shape
    dv = i.shape[-1]
    T = HG_BLOCK
    nB = S // T
    f32 = jnp.float32
    qf = jax.nn.silu(q.astype(f32)) * (dk ** -0.5)
    lbf = lb.astype(f32).reshape(H, dk)
    fg = lbf + (1.0 - lbf) * jax.nn.sigmoid(f.astype(f32))
    kf = 1.0 - fg
    log_f = jnp.log(fg)
    qb = qf.reshape(B, nB, T, H, dk)
    kb = kf.reshape(B, nB, T, H, dk)
    ib = i.astype(f32).reshape(B, nB, T, H, dv)
    Gc = jnp.cumsum(log_f.reshape(B, nB, T, H, dk), axis=2)
    G_last = Gc[:, :, -1:]
    q_in = qb * jnp.exp(Gc)
    k_in = kb * jnp.exp(-Gc)
    k_end = kb * jnp.exp(G_last - Gc)
    A = jnp.einsum('bntha,bnsha->bnhts', q_in, k_in)
    A = jnp.where(jnp.tril(jnp.ones((T, T), dtype=bool)), A, 0.0)
    intra = jnp.einsum('bnhts,bnshe->bnthe', A, ib)

    def step(St, xs):
        q_c, k_c, i_c, dec = xs
        cross = jnp.einsum('btha,bhae->bthe', q_c, St)
        St = St * dec[..., None] + jnp.einsum('btha,bthe->bhae', k_c, i_c)
        return St, cross

    xs = (jnp.moveaxis(q_in, 1, 0), jnp.moveaxis(k_end, 1, 0), jnp.moveaxis(ib, 1, 0),
          jnp.moveaxis(jnp.exp(G_last[:, :, 0]), 1, 0))
    _, cross = lax.scan(step, jnp.zeros((B, H, dk, dv), f32), xs)
    o = (intra + jnp.moveaxis(cross, 0, 1)).reshape(B, S, H * dv)
    o = o * lax.rsqrt(jnp.mean(o * o, axis=-1, keepdims=True) + EPS) * norm_g.astype(f32)
    o = o * jax.nn.silu(og.astype(f32).reshape(B, S, H * dv))
    return o.astype(i.dtype)

def hybrid_mixer(h, w_in, sinks, lb, hg_norm_g, w_branch, w_out, cos, sin):
    B, S, _ = h.shape
    parts = jnp.split(h @ w_in, np.cumsum(IN_SIZES)[:-1].tolist(), axis=-1)
    rq, rk, rv, rg, sq, sk, sv, hq, hf, hi, ho, gates = parts
    y_a = retention(rq.reshape(B, S, RET_HEADS, RET_DK), rk.reshape(B, S, RET_HEADS, RET_DK),
                    rv.reshape(B, S, RET_HEADS, RET_DV), rg.reshape(B, S, RET_HEADS, RET_DV), cos, sin)
    y_b = swa_with_sinks(sq.reshape(B, S, SWA_Q_HEADS, SWA_HD), sk.reshape(B, S, SWA_KV_HEADS, SWA_HD),
                         sv.reshape(B, S, SWA_KV_HEADS, SWA_HD), sinks, cos, sin)
    y_c = hgrn2(hq.reshape(B, S, HG_HEADS, HG_DK), hf.reshape(B, S, HG_HEADS, HG_DK),
                hi.reshape(B, S, HG_HEADS, HG_DV), ho.reshape(B, S, HG_HEADS, HG_DV), lb, hg_norm_g)
    ys = jnp.stack([y_a, y_b, y_c], axis=2)
    yb = jnp.einsum('bsnc,ncd->bsnd', ys, w_branch)
    g = jax.nn.sigmoid(gates.reshape(B, S, N_BRANCH, D_MODEL))
    return jnp.sum(g * yb, axis=2) @ w_out

def mem_xattn(h, m, w_q, w_kv, w_o):
    B, S, _ = h.shape
    M = m.shape[1]
    q = (h @ w_q).reshape(B, S, MEM_HEADS, MEM_HD) * (MEM_HD ** -0.5)
    k, v = jnp.split((m @ w_kv).reshape(B, M, 2 * MEM_HEADS, MEM_HD), 2, axis=2)
    s = jnp.einsum('bshd,bmhd->bhsm', q, k).astype(jnp.float32)
    p = jax.nn.softmax(s, axis=-1).astype(v.dtype)
    o = jnp.einsum('bhsm,bmhd->bshd', p, v).reshape(B, S, MEM_HEADS * MEM_HD)
    return o @ w_o

def conv_ffn(h, w_up, conv_w, conv_b, w_down):
    z = h @ w_up
    S = z.shape[1]
    zp = jnp.pad(z, ((0, 0), (CONV_W - 1, 0), (0, 0)))
    zc = conv_b
    for j in range(CONV_W):
        zc = zc + zp[:, j:j + S] * conv_w[j]
    a, u = jnp.split(zc, 2, axis=-1)
    return (jax.nn.silu(a) * u) @ w_down

def setup_inputs(seed: int = 0) -> dict:
    key = jax.random.key(seed)
    ks = jax.random.split(key, 24)
    f32 = jnp.float32

    def w(k, shape, fan_in):
        return jax.random.normal(k, shape, f32) * (fan_in ** -0.5)

    def gain(k, shape):
        return 1.0 + 0.02 * jax.random.normal(k, shape, f32)

    positions = (jnp.arange(SEQ, dtype=jnp.int32)[None, :]
                 + CHUNK * jax.random.randint(ks[2], (BATCH, 1), 0, 64, dtype=jnp.int32))
    return {
        "x": jax.random.normal(ks[0], (BATCH, SEQ, D_MODEL), f32),
        "mem": jax.random.normal(ks[1], (BATCH, MEM_LEN, D_MODEL), f32),
        "positions": positions,
        "norm_mix_g": gain(ks[3], (DEPTH, D_MODEL)),
        "w_in": w(ks[4], (DEPTH, D_MODEL, IN_COLS), D_MODEL),
        "swa_sinks": 0.5 * jax.random.normal(ks[5], (DEPTH, SWA_Q_HEADS), f32),
        "hg_lb_logits": jax.random.normal(ks[6], (DEPTH, HG_HEADS * HG_DK), f32),
        "hg_norm_g": gain(ks[7], (DEPTH, HG_HEADS * HG_DV)),
        "w_branch": w(ks[8], (DEPTH, N_BRANCH, BRANCH_W, D_MODEL), BRANCH_W),
        "w_out": w(ks[9], (DEPTH, D_MODEL, D_MODEL), D_MODEL),
        "norm_mem_g": gain(ks[10], (DEPTH, D_MODEL)),
        "mem_norm_g": gain(ks[11], (DEPTH, D_MODEL)),
        "w_mq": w(ks[12], (DEPTH, D_MODEL, MEM_HEADS * MEM_HD), D_MODEL),
        "w_mkv": w(ks[13], (DEPTH, D_MODEL, 2 * MEM_HEADS * MEM_HD), D_MODEL),
        "w_mo": w(ks[14], (DEPTH, MEM_HEADS * MEM_HD, D_MODEL), MEM_HEADS * MEM_HD),
        "norm_ffn_g": gain(ks[15], (DEPTH, D_MODEL)),
        "w_up": w(ks[16], (DEPTH, D_MODEL, 2 * D_FF), D_MODEL),
        "conv_w": w(ks[17], (DEPTH, CONV_W, 2 * D_FF), CONV_W),
        "conv_b": 0.01 * jax.random.normal(ks[18], (DEPTH, 2 * D_FF), f32),
        "w_down": w(ks[19], (DEPTH, D_FF, D_MODEL), D_FF),
        "final_norm_g": gain(ks[20], (D_MODEL,)),
    }

def reference(x, mem, positions, norm_mix_g, w_in, swa_sinks, hg_lb_logits, hg_norm_g, w_branch,
              w_out, norm_mem_g, mem_norm_g, w_mq, w_mkv, w_mo, norm_ffn_g, w_up, conv_w, conv_b,
              w_down, final_norm_g):
    cos, sin = rope_tables(positions, SWA_HD)
    lb_sm = jax.nn.softmax(hg_lb_logits.astype(jnp.float32), axis=0)
    lb_all = jnp.cumsum(lb_sm, axis=0) - lb_sm[0:1]
    for l in range(DEPTH):
        h = rms_norm(x, norm_mix_g[l])
        x = x + hybrid_mixer(h, w_in[l], swa_sinks[l], lb_all[l], hg_norm_g[l], w_branch[l],
                             w_out[l], cos, sin)
        h = rms_norm(x, norm_mem_g[l])
        x = x + mem_xattn(h, rms_norm(mem, mem_norm_g[l]), w_mq[l], w_mkv[l], w_mo[l])
        h = rms_norm(x, norm_ffn_g[l])
        x = x + conv_ffn(h, w_up[l], conv_w[l], conv_b[l], w_down[l])
    return rms_norm(x, final_norm_g)


_drawn_inputs = setup_inputs


def setup_inputs(seed=0):
    import zlib

    import numpy as np

    out = dict(_drawn_inputs(seed))
    spreads = {}
    factors = {'norm_mix_g': 3.476,
     'swa_sinks': 64.0,
     'hg_norm_g': 8.0,
     'norm_mem_g': 8.0,
     'mem_norm_g': 8.0,
     'norm_ffn_g': 13.243,
     'conv_b': 26.127,
     'final_norm_g': 8.663}
    for name, (base, spread) in spreads.items():
        noise = np.random.default_rng([zlib.crc32(name.encode()), seed]).standard_normal(out[name].shape)
        drawn = base * np.exp(spread * noise) if base else spread * noise
        out[name] = __import__('jax').numpy.asarray(drawn.astype(out[name].dtype))
    for name, factor in factors.items():
        out[name] = (out[name] * factor).astype(out[name].dtype)
    return out
```

```python
from contextlib import ExitStack

import numpy as np

import concourse.bass as bass
from concourse import mybir

ALU = mybir.AluOpType
ACT = mybir.ActivationFunctionType
F32 = mybir.dt.float32
F32R = mybir.dt.float32r
I32 = mybir.dt.int32
U32 = mybir.dt.uint32
AX_X = mybir.AxisListType.X

P = 128
D = 1024
S = 512
KD = D // P
NT = S // P
EPS = 1e-6
L = 64
BR = 512
KB = BR // P
FF = 2816
KF = FF // P
M = 256
MT = M // P
H = 4
HG_T = 16

C_RQ, C_RK, C_RV, C_RG = 0, 256, 512, 1024
C_SQ, C_SK = 1536, 2048
C_HQ, C_HF, C_HI, C_HO = 2304, 2816, 3328, 3840
C_GATE = 4352

PAIRS = [C_HF, C_HF + 256, C_HQ, C_HQ + 256, C_HI, C_HI + 256, C_HO, C_HO + 256,
         C_RQ, C_RK, C_RV, C_RV + 256, C_RG, C_RG + 256, C_SQ, C_SQ + 256, C_SK]
N_G0 = len(PAIRS)
N_G1 = N_G0 + KD
N_LINE = N_G1 + 2
N_G2 = N_G1 + KD
N_OUT = N_G2 + KD
N_MK = N_OUT + 4
N_MQ = N_MK + 2
N_MV = N_MQ + 2
N_MO = N_MV + 2
N_UP = N_MO + 4
N_DN = N_UP + KF
KH = KF // 2

K_ID = 0
K_MASK = K_ID + P
K_DECAY = K_MASK + 4 * P
K_INV = K_DECAY + H * S
K_ALL = K_INV + 32

R_CONV = 0
R_GAIN = 4 * 2 * KF
R_HG = R_GAIN + 5 * KD
R_ALL = R_HG + 2 * H
G_MIX, G_MEM, G_MEMN, G_FFN, G_FIN = (R_GAIN + KD * i for i in range(5))

MAGIC = 12582912.0


def split_two_pi():
    parts, rest = [], 2 * np.pi
    for _ in range(3):
        scale = 2.0 ** (11 - int(np.floor(np.log2(abs(rest)))))
        part = np.round(rest * scale) / scale
        parts.append(float(part))
        rest -= part
    return parts


class Slot:

    def __init__(self, c, i=None, per=0):
        self.c, self.i, self.per = c, i, per
        self.s = c % 2

    def __add__(self, k):
        return Slot(self.c + k, self.i, self.per)

    def n(self, k=0):
        return self.c + k if self.i is None else self.i * self.per + (self.c + k)

    def loads(self):
        c = 32 * (self.c // 2 + 1)
        return c if self.i is None else self.i * (16 * self.per) + c


class Order:

    def __init__(self, eng, own):
        self.eng, self.own, self.count, self.i, self.per = eng, own, {}, None, {}

    def sig(self, ins, sem=None):
        sem = self.own if sem is None else sem
        ins.then_inc(sem, 1)
        self.last = sem
        self.count[sem.name] = self.count.get(sem.name, 0) + 1

    def settle(self):
        n = self.count[self.last.name]
        per = self.per.get(self.last.name, 0)
        self.eng.wait_ge(self.last, n if self.i is None or not per else self.i * per + n)

    def enter(self, i, per):
        self.i, self.per, self.base = i, {s.name: k for s, k in per}, dict(self.count)

    def leave(self, turns):
        for name, n in self.count.items():
            k = n - self.base.get(name, 0)
            assert k == self.per.get(name, 0), (name, k)
            self.count[name] = n + k * (turns - 1)
        self.i, self.per = None, {}


def hybrid_layer(nc, x, mem, positions, norm_mix_g, w_in, swa_sinks, hg_lb_logits, hg_norm_g, w_branch,
                 w_out, norm_mem_g, mem_norm_g, w_mq, w_mkv, w_mo, norm_ffn_g, w_up, conv_w, conv_b,
                 w_down, final_norm_g, consts, out):
    ctx = ExitStack()
    with ctx:
        KIB = 1024
        base = [(nc.sbuf_base + 63) // 64 * 64]

        def at(name, offset, shape, dt=F32):
            return nc.alloc_sbuf_tensor_at(name, shape, dt, offset=offset)

        def fixed(name, shape, dt=F32):
            t = at(name, base[0], shape, dt)
            base[0] += (int(np.prod(shape[1:])) * 4 + 31) // 32 * 32
            return t

        H_AT = base[0]
        hH = fixed("hH", [P, KD, S], F32R)
        hL = fixed("hL", [P, KD, S], F32R)
        raw = [fixed(f"raw{s}", [P, 2048]) for s in range(2)]
        wH = [fixed(f"wH{s}", [P, 2048], F32R) for s in range(2)]
        wL = [fixed(f"wL{s}", [P, 2048], F32R) for s in range(2)]
        ident = fixed("ident", [P, P])
        ones = fixed("ones", [P, 8])
        par = fixed("par", [P, R_ALL])
        rstd_row = fixed("rstd_row", [P, S])
        rstd = fixed("rstd", [P, 2 * NT])
        eps = fixed("eps", [P, 8])
        ssq = fixed("ssq", [P, 8])
        U0 = base[0]
        A = U0 + 16 * KIB
        U = [U0, U0 + 8 * KIB] + [A + 8 * KIB * i for i in range(6)]
        U_AT = A + 48 * KIB
        U_R = U_AT + 20 * KIB
        U_C = U_R + 16 * KIB

        masks = at("masks", U_C, [P, 4, P])
        decay = at("decay", U_C + 2 * KIB, [P, H, S])
        cosT = at("cosT", U_C + 10 * KIB, [P, S])
        sinT = at("sinT", U_C + 12 * KIB, [P, S])
        sv = at("sv", U_C + 14 * KIB, [P, NT, P])
        sk = at("sk", U_C + 16 * KIB, [P, S])
        restart = at("restart", U_C + 16 * KIB, [P, S])
        T = U_C + 18 * KIB
        e16 = at("e16", T, [P, H, 32])
        e32 = at("e32", T + 512, [P, H, 16])
        e64 = at("e64", T + 768, [P, H, 8])
        e128 = at("e128", T + 896, [P, H, 4])
        lb = at("lb", T + 960, [P, 2, H])
        lbt = at("lbt", T + 992, [P, 2, H])
        stat = at("stat", T + 1024, [P, 16])
        statr = at("statr", T + 1088, [P, 16])
        sinks = at("sinks", T + 1152, [P, 2, 2])
        sink16 = at("sink16", T + 1184, [P, 2, 2, 2, 2])
        smx = at("smx", T + 1248, [P, 2, 16])
        snk = at("snk", T + 1376, [P, 2, 16])
        ssum = at("ssum", T + 1504, [P, 2, 16])
        invf = at("invf", T + 1632, [P, 32])
        mstat = at("mstat", T + 1760, [P, 4, H, NT])
        memst = at("memst", T + 2016, [P, 8])
        assert T + 2048 <= nc.sbuf_usable_end

        xtok = at("xtok", U_R, [P, NT, D])
        junk = at("junk", U[0], [P, D])
        rows_conv = at("rows_conv", U[2], [2 * KF, 4, P])
        rows_gain = at("rows_gain", U[2] + 2 * KIB, [KD, 5, P])
        rows_hg = at("rows_hg", U[2] + 5 * KIB, [H, 2, P])
        posi = at("posi", U[3], [P, NT], I32)
        posf = at("posf", U[3] + 32, [P, NT])
        ang = at("ang", U[3] + 1024, [P, NT, 32])
        turn = at("turn", U[3] + 1536, [P, NT, 32])
        trig = at("trig", U[3] + 2048, [P, 2, NT, 32])
        wide = at("wide", U[3] + 4096, [P, 2, NT, 4, 32])

        hgF = at("hgF", U[0], [P, H, S])
        hgQ = at("hgQ", U[1], [P, H, S])
        hgK = at("hgK", U[2], [P, H, S])
        hgG = at("hgG", U[3], [P, H, S])
        hgk = at("hgk", U[4], [P, H, S])
        hgl = at("hgl", U_R, [P, H, S])
        hgO = at("hgO", U[5], [P, H, S])
        hgV = at("hgV", U[6], [P, NT, BR])
        hgY = at("hgY", U[1], [P, H, S])
        hgsq = at("hgsq", U[0], [P, H, S])
        att = [at(f"att{i}", U_AT + o * KIB, [P, H, S - P * i]) for i, o in enumerate((0, 8, 14, 18))]
        ycH = at("ycH", U_R, [P, KB, S], F32R)
        ycL = at("ycL", U_R + 8 * KIB, [P, KB, S], F32R)
        rqk = at("rqk", U[2], [P, 4, S])
        rsw = at("rsw", U[4], [P, 4, S])
        rV = at("rV", U[3], [P, NT, BR])
        rG = at("rG", U[7], [P, H, S])
        rY = at("rY", U[4], [P, H, S])
        rsq = at("rsq", U[2], [P, H, S])
        yaH = at("yaH", U[2], [P, KB, S], F32R)
        yaL = at("yaL", U[3], [P, KB, S], F32R)
        sq = at("sq", U[6], [P, 4, S])
        sqc = at("sqc", U[5], [P, 2, S // L, 2, L])
        ssw = at("ssw", U_AT, [P, 4, S])
        ssk = at("ssk", U_AT + 8 * KIB, [P, S])
        kd = at("kd", U_AT + 12 * KIB, [P, 2, S])
        vb = at("vb", U_AT + 16 * KIB, [P, NT, P])
        sP = [at("sP0", U[7], [P, 16, P]), at("sP1", U_AT, [P, 16, P])]
        sPT = at("sPT", U[6], [P, 16, P])
        ybH = at("ybH", U[5], [P, KB, S], F32R)
        ybL = at("ybL", U[7], [P, KB, S], F32R)
        mix = at("mix", U0, [P, KD, S])
        mixH = at("mixH", U[2], [P, KD, S], F32R)
        mixL = at("mixL", U_AT, [P, KD, S], F32R)
        gate = [at(f"gate{s}", U_C + (2 + 2 * s) * KIB, [P, S]) for s in range(2)]
        gmix = at("gmix", U_C + 6 * KIB, [P, S])
        xT = at("xT", U0, [P, KD, S])
        xtok2 = at("xtok2", U_R, [P, NT, D])
        sqr = at("sqr", U_C + 8 * KIB, [P, S])
        ssqT = at("ssqT", U[4] + 4 * KIB, [P, S])
        memtok = at("memtok", U[4], [P, MT, D])
        mjunk = at("mjunk", U_AT + 8 * KIB, [P, D])
        memH = at("memH", U_C + 10 * KIB, [P, KD, M], F32R)
        memL = at("memL", U[6], [P, KD, M], F32R)
        mkT = at("mkT", U_AT + 16 * KIB, [P, H, M])
        mV = at("mV", U[4], [P, MT, BR])
        mq = at("mq", U[5], [P, H, S])
        mP = [at(f"mP{i}", U[7] + 4 * KIB * i, [P, NT, M]) for i in range(2)]
        mPT = [at(f"mPT{i}", U[2] + 4 * KIB * i, [P, MT, S]) for i in range(2)]
        moH = at("moH", U[3], [P, H, S], F32R)
        moL = at("moL", U_AT, [P, H, S], F32R)
        actH = at("actH", A, [P, KF, S], F32R)
        actL = at("actL", A + 44 * KIB, [P, KF, S], F32R)
        B = A + 88 * KIB
        za = at("za", B, [P, S + 2])
        zu = at("zu", B + 2080, [P, S + 2])
        ca = at("ca", B + 4160, [P, S])
        cu = at("cu", B + 4160 + 2 * KIB, [P, S])
        prod = at("prod", B + 4160 + 4 * KIB, [P, S])
        fsq = at("fsq", B + 4160 + 6 * KIB, [P, S])
        xg = at("xg", B + 4160 + 8 * KIB, [P, S])
        ssqF = at("ssqF", B + 4160 + 10 * KIB, [P, S])
        assert B + 4160 + 12 * KIB <= nc.sbuf_usable_end
        otok = at("otok", H_AT, [P, NT, D])

        ps = ctx.enter_context(nc.psum_tensor("ps", [P, 8, S], F32))

        def sems(names):
            return [ctx.enter_context(nc.semaphore(name)) for name in names.split()]

        raw_in = sems("raw_in0 raw_in1")
        ident_in, const_in, x_in, par_in, mem_in, x2_in, out_done = sems(
            "ident_in const_in x_in par_in mem_in x2_in out_done")
        hi_ready, lo_ready, first_done, slot_done, taken = sems("hi_ready lo_ready first_done slot_done taken")
        dve_step, act_step, pool_step = sems("dve_step act_step pool_step")
        (set_up, att_zero, par_T, par_ready, std_ready, rstd_ready, xT_out, h_hi, h_ready, row_out, lb_arg,
         lb_exp, ang_ready, sin_ready, wide_ready, tab_out, tab_ready) = sems(
             "set_up att_zero par_T par_ready std_ready rstd_ready xT_out h_hi h_ready row_out lb_arg "
             "lb_exp ang_ready sin_ready wide_ready tab_out tab_ready")
        (hg_sig, hg_arg, hg_ln, hg_G, hg_eG, hg_e16, hg_qs, hg_qin, hg_enG, hg_diff, hg_ed, hg_kq, hg_og,
         lev_out, lev_kq, lev_taken, hg_o, hg_sq, hg_ms, hg_std, hg_rs, hg_row, hg_yf, hg_hi, yc_ready) = sems(
             "hg_sig hg_arg hg_ln hg_G hg_eG hg_e16 hg_qs hg_qin hg_enG hg_diff hg_ed hg_kq hg_og "
             "lev_out lev_kq lev_taken hg_o hg_sq hg_ms hg_std hg_rs hg_row hg_yf hg_hi yc_ready")
        (r_sw, r_rope, r_sc, r_att, r_g, r_o, r_sqd, r_ms, r_std, r_rs, r_row, r_yf, r_hi, ya_ready) = sems(
            "r_sw r_rope r_sc r_att r_g r_o r_sqd r_ms r_std r_rs r_row r_yf r_hi ya_ready")
        (s_sw, s_rope, s_kd, s_sc, s_arg, s_exp, s_prob, s_T, s_PT, s_o, s_hi, yb_ready) = sems(
            "s_sw s_rope s_kd s_sc s_arg s_exp s_prob s_T s_PT s_o s_hi yb_ready")
        g_in, g_sig, mix_sum, mix_hi, mix_ready = sems("g_in g_sig mix_sum mix_hi mix_ready")
        m_std, m_rs, m_norm, m_T, m_hi, m_ready = sems("m_std m_rs m_norm m_T m_hi m_ready")
        x_new, x_hi, x_sq, x_lo, x_acc, n_ms, n_std, n_rs, n_row, n_ready = sems(
            "x_new x_hi x_sq x_lo x_acc n_ms n_std n_rs n_row n_ready")
        a_sc, a_max, a_exp, a_prob, a_T, a_PT, a_o, a_hi, a_ready = sems(
            "a_sc a_max a_exp a_prob a_T a_PT a_o a_hi a_ready")
        f_conv, f_silu, f_prod, f_hi, f_ready = sems("f_conv f_silu f_prod f_hi f_ready")
        o_new, o_sq, o_g, o_acc, o_T, o_tok, o_ms, o_std, o_rs, o_fin = sems(
            "o_new o_sq o_g o_acc o_T o_tok o_ms o_std o_rs o_fin")

        block = ctx.enter_context(nc.Block())

        @block.sync
        def _(sp):
            def kp(w):
                return w.rearrange("(k p) c -> p k c", p=P)

            win, wout, wmq, wmkv = kp(w_in[0]), kp(w_out[0]), kp(w_mq[0]), kp(w_mkv[0])
            wmo, wup, wdn = kp(w_mo[0]), kp(w_up[0]), kp(w_down[0])
            wbr = [kp(w_branch[0, b]) for b in range(3)]

            def load(n, *pieces):
                if n.c >= 2:
                    sp.wait_ge(lo_ready, n.n(-1))
                for dst, src in pieces:
                    sp.dma_start(dst, src).then_inc(raw_in[n.s], 16)

            def load_pair(n, w, c0):
                v = raw[n.s][:, :].rearrange("p (k c) -> p k c", k=KD)
                load(n, *((v[:, k:k + 4, :], w[:, k:k + 4, bass.ds(c0, 256)]) for k in (0, 4)))

            def load_gate(n, b, j):
                v = raw[n.s][:, 0:12 * P].rearrange("p (k c) -> p k c", k=12)
                load(n, (v[:, 0:8, :], win[:, :, bass.ds(j * P + (C_GATE + b * D), P)]),
                     (v[:, 8:12, :], wbr[b][:, :, bass.ds(j * P, P)]))

            def load_mo(n, c0):
                v = raw[n.s][:, 0:4 * 256].rearrange("p (k c) -> p k c", k=4)
                load(n, *((v[:, k:k + 2, :], wmo[:, k:k + 2, bass.ds(c0, 256)]) for k in (0, 2)))

            def load_up(n, j):
                v = raw[n.s][:, :].rearrange("p (k h c) -> p h k c", k=KD, h=2)
                load(n, *((v[:, h], wup[:, :, bass.ds(j * P + h * FF, P)]) for h in (0, 1)))

            def load_down(n, j, half):
                v = raw[n.s][:, 0:KH * P].rearrange("p (k c) -> p k c", k=KH)
                load(n, *((v[:, a:b, :], wdn[:, KH * half + a:KH * half + b, bass.ds(j * P, P)])
                          for a, b in ((0, 6), (6, KH))))

            xsrc = x[0].rearrange("(t p) d -> p t d", p=P)
            sp.dma_start(ident[:, :], consts[:, K_ID:K_ID + P]).then_inc(ident_in, 16)
            for t in range(NT):
                sp.dma_start(xtok[:, t, :], xsrc[:, t, :]).then_inc(x_in, 16)
            sp.dma_start(rows_gain[:, 0, :], norm_mix_g[0].rearrange("(k p) -> k p", p=P)).then_inc(par_in, 16)
            sp.dma_start(rows_gain[:, 1, :], norm_mem_g[0].rearrange("(k p) -> k p", p=P)).then_inc(par_in, 16)
            sp.dma_start(rows_gain[:, 2, :], mem_norm_g[0].rearrange("(k p) -> k p", p=P)).then_inc(par_in, 16)
            sp.dma_start(rows_gain[:, 3, :], norm_ffn_g[0].rearrange("(k p) -> k p", p=P)).then_inc(par_in, 16)
            sp.dma_start(rows_gain[:, 4, :], final_norm_g.rearrange("(k p) -> k p", p=P)).then_inc(par_in, 16)
            sp.dma_start(rows_hg[:, 0, :], hg_norm_g[0].rearrange("(k p) -> k p", p=P)).then_inc(par_in, 16)
            sp.dma_start(rows_hg[:, 1, :], hg_lb_logits[0].rearrange("(k p) -> k p", p=P)).then_inc(par_in, 16)
            sp.dma_start(rows_conv[:, 0:3, :],
                         conv_w[0].rearrange("j (k p) -> k j p", p=P)).then_inc(par_in, 16)
            sp.dma_start(rows_conv[:, 3, :], conv_b[0].rearrange("(k p) -> k p", p=P)).then_inc(par_in, 16)
            load_pair(Slot(0), win, PAIRS[0])
            sp.dma_start(posi[:, :], positions[0].rearrange("(t p) -> p t", p=P),
                         allow_slow_non_contiguous=True).then_inc(const_in, 16)
            sp.dma_start(invf[:, :], consts[:, K_INV:K_INV + 32]).then_inc(const_in, 16)
            load_pair(Slot(1), win, PAIRS[1])
            sp.dma_start(masks[:, :, :],
                         consts[:, K_MASK:K_MASK + 4 * P].rearrange("p (i t) -> p i t", i=4)).then_inc(const_in, 16)
            sp.dma_start(decay[:, :, :],
                         consts[:, K_DECAY:K_DECAY + H * S].rearrange("p (h t) -> p h t", h=H)).then_inc(const_in, 16)
            sk4 = swa_sinks[0].rearrange("(v a r) -> a r v", v=2, a=2)
            for a in range(2):
                for r in range(2):
                    sp.dma_start(sinks[64 * a:64 * a + 64, r, :], sk4[a, r].partition_broadcast(64),
                                 allow_slow_non_contiguous=True).then_inc(const_in, 16)
            for c in range(2, N_G0):
                load_pair(Slot(c), win, PAIRS[c])
            for c in range(N_G0, N_LINE):
                load_gate(Slot(c), 2 if c < N_G1 else 0, (c - N_G0) % KD)
                if c == N_G0 + 8:
                    sp.wait_ge(ya_ready, 1)
                    sp.dma_start(memtok[:, :, :], mem[0].rearrange("(t p) d -> p t d", p=P)).then_inc(mem_in, 16)
            sp.wait_ge(slot_done, N_G1)
            sp.dma_start(xtok2[:, :, :], xsrc).then_inc(x2_in, 16)
            with sp.Fori(0, (N_G2 - N_LINE) // 2) as i:
                for k in range(2):
                    load_gate(Slot(N_LINE + k, i, 2), 0, i * 2 + (2 + k))
            with sp.Fori(0, KD // 2) as i:
                for k in range(2):
                    load_gate(Slot(N_G2 + k, i, 2), 1, i * 2 + k)
            for c in range(4):
                load_pair(Slot(N_OUT + c), wout, 256 * c)
            for c in range(2):
                load_pair(Slot(N_MK + c), wmkv, 256 * c)
            for c in range(2):
                load_pair(Slot(N_MQ + c), wmq, 256 * c)
            for c in range(2):
                load_pair(Slot(N_MV + c), wmkv, BR + 256 * c)
            with sp.Fori(0, 2) as i:
                for k in range(2):
                    load_mo(Slot(N_MO + k, i, 2), i * 512 + 256 * k)
            with sp.Fori(0, KF // 2) as i:
                for k in range(2):
                    load_up(Slot(N_UP + k, i, 2), i * 2 + k)
            with sp.Fori(0, KD) as i:
                for k in range(2):
                    load_down(Slot(N_DN + k, i, 2), i, k)
            osrc = out[0].rearrange("(t p) d -> p t d", p=P)
            for t in range(NT):
                sp.wait_ge(o_fin, t + 1)
                sp.dma_start(osrc[:, t, :], otok[:, t, :]).then_inc(out_done, 16)
            sp.wait_ge(out_done, 16 * NT)

        @block.gpsimd
        def _(pool):
            for i in range(NT):
                pool.memset(att[i][:, :, :], 0.0).then_inc(att_zero, 1)

        @block.tensor
        def _(pe):
            def product(out_ap, terms, done=None, start=True, stop=True):
                passes = [(a, b) for lh, ll, rh, rl in terms for a, b in ((lh, rh), (lh, rl), (ll, rh))]
                for m, (a, b) in enumerate(passes):
                    last = pe.matmul(out_ap, a, b, start=start and m == 0, stop=stop and m == len(passes) - 1)
                if done is not None:
                    last.then_inc(done, 1)
                return last

            def enter(n, banks=True):
                pe.wait_ge(lo_ready, n.n(1))
                if banks and n.c >= 2:
                    pe.wait_ge(taken, n.n(-1))

            def weights(n, k, kt, cols):
                return (wH[n.s][:, 0:kt * cols].rearrange("p (k c) -> p k c", k=kt),
                        wL[n.s][:, 0:kt * cols].rearrange("p (k c) -> p k c", k=kt))

            def tile_product(n, c, kt, cols, k0, k1, xh, xl, done, xk0=0, width=S):
                vh, vl = weights(n, None, kt, cols)
                b = 2 * n.s + c
                cc = P * c if cols > P else 0
                product(ps[:, b, 0:width],
                        [(vh[:, k, cc:cc + P], vl[:, k, cc:cc + P], xh[:, k - xk0, 0:width], xl[:, k - xk0, 0:width])
                         for k in range(k0, k1)], done)

            def pair_T(n, xh, xl, kt=KD, width=S):
                enter(n)
                tile_product(n, 0, kt, 256, 0, kt, xh, xl, first_done, 0, width)
                tile_product(n, 1, kt, 256, 0, kt, xh, xl, slot_done, 0, width)

            def pair_V(n, xh, xl, tiles=NT):
                enter(n)
                vh, vl = weights(n, None, KD, 256)
                for t in range(tiles):
                    b = 2 * n.s + (t // 2 if tiles == NT else t)
                    c0 = 256 * (t % 2) if tiles == NT else 0
                    f = slice(P * t, P * t + P)
                    done = {tiles // 2 - 1: first_done, tiles - 1: slot_done}.get(t)
                    product(ps[:, b, c0:c0 + 256],
                            [(xh[:, k, f], xl[:, k, f], vh[:, k, :], vl[:, k, :]) for k in range(KD)], done)

            def transposes(bank, blocks, done):
                for out_ap, in_ap in blocks:
                    k = in_ap.shape[0]
                    last = pe.transpose(out_ap, in_ap, ident[0:k, 0:k])
                last.then_inc(done, 1)

            def rows_of(cols, bank, done):
                for t in range(NT):
                    last = pe.matmul(ps[:, bank, P * t:P * t + P], cols[:, t:t + 1].to_broadcast([P, P]), ident[:, :],
                                     start=True, stop=True)
                last.then_inc(done, 1)

            def column_sums(groups, bank, done):
                for c, tiles in enumerate(groups):
                    for m, a in enumerate(tiles):
                        last = pe.matmul(ps[:, bank, c:c + 1], a, ones[:, 0:1], start=m == 0,
                                         stop=m == len(tiles) - 1)
                last.then_inc(done, 1)

            pe.wait_ge(ident_in, 16)
            pe.wait_ge(par_in, 9 * 16)
            blocks = [(ps[:, 0, R_CONV + 2 * KF * i:R_CONV + 2 * KF * (i + 1)], rows_conv[:, i, :]) for i in range(4)]
            blocks += [(ps[:, 0, R_GAIN + KD * i:R_GAIN + KD * (i + 1)], rows_gain[:, i, :]) for i in range(5)]
            blocks += [(ps[:, 0, R_HG + H * i:R_HG + H * (i + 1)], rows_hg[:, i, :]) for i in range(2)]
            transposes(0, blocks, par_T)
            pe.wait_ge(x_in, 16 * NT)
            for k in range(KD):
                b = (k + 1) % 8
                if b == 0:
                    pe.wait_ge(par_ready, 1)
                transposes(b, [(ps[:, b, P * t:P * t + P], xtok[:, t, P * k:P * k + P]) for t in range(NT)], xT_out)
            pe.wait_ge(h_ready, KD)

            def levels(li, ks, banks_free):
                for i in range(NT):
                    pe.wait_ge(lev_taken, banks_free + i + 1)
                    for h in range(H):
                        f = slice(P * i, P * i + P)
                        last = pe.matmul(ps[:, 4 + i, P * h:P * h + P], ks[:, h, f], hgQ[:, h, f],
                                         start=True, stop=True)
                    last.then_inc(lev_out, 1)

            def values(v, done):
                for h in range(H):
                    for i in range(NT):
                        last = pe.matmul(ps[:, 4 + h, P * i:S], v[:, i, P * h:P * h + P], att[i][:, h, :],
                                         start=i == 0, stop=i == NT - 1)
                    last.then_inc(done, 1)

            def r_scores(h, i, bank, c0):
                r = slice(64 * (h % 2), 64 * (h % 2) + 64)
                return pe.matmul(ps[:, bank, c0:c0 + S - P * i], rqk[r, 2 + h // 2, P * i:P * i + P],
                                 rqk[r, h // 2, P * i:S], start=True, stop=True)

            def s_scores(hf):
                for cp in range(2):
                    for r in range(2):
                        rows = slice(64 * r, 64 * r + 64)
                        for cm in range(2):
                            c = 4 * hf + 2 * cp + cm
                            for v in range(2):
                                q = sqc[rows, v, c].rearrange("p a t -> p (a t)")
                                o = ps[:, 4 + 2 * cp + r, 256 * cm + 128 * v:256 * cm + 128 * v + 128]
                                if cm:
                                    last = pe.matmul(o, q, kd[rows, v, L * (c - 1):L * (c + 1)], start=True, stop=True)
                                else:
                                    odd = max(c - 1, 0)
                                    pe.matmul(o[:, 0:L], q, kd[rows, v, L * c:L * c + L], start=True, stop=True)
                                    last = pe.matmul(o[:, L:2 * L], q, kd[rows, v, L * odd:L * odd + L],
                                                     start=True, stop=True)
                last.then_inc(s_sc, 1)

            def s_values(hf):
                for u in range(16):
                    cp, r, cm, v = u // 8, u // 4 % 2, u // 2 % 2, u % 2
                    c = 4 * hf + 2 * cp + cm
                    band = sv[:, c // 2, :] if cm else vb[:, c // 2, :]
                    k = L if c == 0 else P
                    o = ps[64 * r:64 * r + 64, 4 + v, :].rearrange("p (a t) -> p a t", a=2)
                    last = pe.matmul(o[:, :, L * (c % 4):L * (c % 4) + L], band[0:k, 64 * v:64 * v + 64],
                                     sPT[0:k, u, :].rearrange("p (a t) -> p a t", a=2), start=True, stop=True)
                last.then_inc(s_o, 1)

            def job(n):
                if n == 0:
                    pe.wait_ge(rstd_ready, 1)
                    rows_of(rstd, 4, row_out)
                    pe.wait_ge(wide_ready, 1)
                    for i in range(2):
                        transposes(5 + i, [(ps[:, 5 + i, P * t:P * t + P],
                                            wide[:, i, t].rearrange("p q f -> p (q f)")) for t in range(NT)], tab_out)
                elif n == 5:
                    pe.wait_ge(hg_kq, 2)
                    pe.wait_ge(tab_ready, 2)
                    for i in range(NT):
                        for h in range(H):
                            f = slice(P * i, P * i + P)
                            last = pe.matmul(ps[:, 4 + i, P * h:P * h + P], hgK[:, h, f], hgQ[:, h, f],
                                             start=True, stop=True)
                        last.then_inc(lev_out, 1)
                elif n == 6:
                    levels(1, hgF, 0)
                elif n == 7:
                    pe.wait_ge(lev_kq, 1)
                    levels(2, hgF, 4)
                elif n == 8:
                    pe.wait_ge(lev_kq, 2)
                    levels(3, hgF, 8)
                elif n == 9:
                    pe.wait_ge(lev_kq, 3)
                    for m, i in enumerate((0, 2)):
                        pe.wait_ge(lev_taken, 13 + m)
                        for h in range(H):
                            last = pe.matmul(ps[:, 4 + m, P * h:P * h + P], hgF[:, h, P * i:P * i + P],
                                             hgQ[:, h, P * i + P:P * i + 2 * P], start=True, stop=True)
                        last.then_inc(lev_out, 1)
                elif n == 10:
                    pe.wait_ge(lev_kq, 4)
                    pe.wait_ge(lev_taken, 18)
                    for m in range(4):
                        i = m // 2
                        for h in (2 * (m % 2), 2 * (m % 2) + 1):
                            last = pe.matmul(ps[:, 4 + m, 256 * (h % 2):256 * (h % 2) + 256],
                                             hgF[:, h, P * i:P * i + P], hgQ[:, h, 2 * P:S], start=True, stop=True)
                        last.then_inc(lev_out, 1)
                elif n == 11:
                    pe.wait_ge(lev_taken, 22)
                    values(hgV, hg_o)
                elif n == 12:
                    pe.wait_ge(hg_sq, H)
                    column_sums([[hgsq[:, h, P * t:P * t + P] for h in range(H)] for t in range(NT)], 4, hg_ms)
                elif n == 13:
                    pe.wait_ge(hg_rs, 1)
                    rows_of(statr, 4, hg_row)
                elif n == 14:
                    pe.wait_ge(hg_yf, 1)
                    pe.wait_ge(r_rope, 1)
                    for h in range(H):
                        r_scores(h, 0, 4 + h, 0).then_inc(r_sc, 1)
                elif n == 15:
                    for h in range(H):
                        pe.wait_ge(r_att, h + 1)
                        r_scores(h, 1, 4 + h, 0).then_inc(r_sc, 1)
                elif n == 16:
                    pe.wait_ge(r_att, 8)
                    for i, b0 in ((2, 4), (3, 6)):
                        for r in range(2):
                            r_scores(r, i, b0 + r, 0)
                            r_scores(r + 2, i, b0 + r, 256).then_inc(r_sc, 1)
                elif n == 17:
                    pe.wait_ge(r_att, 12)
                    values(rV, r_o)
                elif n == 18:
                    pe.wait_ge(r_sqd, H)
                    column_sums([[rsq[:, h, P * t:P * t + P]] for h in range(H) for t in range(NT)], 4, r_ms)
                elif n == 19:
                    pe.wait_ge(r_rs, 1)
                    for h in range(H):
                        rows_of(statr[:, 4 * h:4 * h + 4], 4 + h, r_row)
                elif n == 20:
                    pe.wait_ge(r_yf, 1)
                    pe.wait_ge(s_rope, 1)
                    pe.wait_ge(s_kd, 1)
                    s_scores(0)
                elif n == 21:
                    pe.wait_ge(s_arg, 1)
                    s_scores(1)
                elif n in (22, 24):
                    hf = (n - 22) // 2
                    pe.wait_ge(s_arg, 2)
                    pe.wait_ge(s_prob, hf + 1)
                    if hf:
                        pe.wait_ge(yb_ready, 1)
                    for b in range(4):
                        transposes(4 + b, [(ps[:, 4 + b, P * (u % 4):P * (u % 4) + P], sP[hf][:, u, :])
                                           for u in range(4 * b, 4 * b + 4)], s_T)
                elif n in (23, 25):
                    hf = (n - 23) // 2
                    pe.wait_ge(s_PT, 4 * hf + 4)
                    s_values(hf)
                elif n == 26:
                    pe.wait_ge(m_norm, 1)
                    pe.wait_ge(yb_ready, 2)
                    for b in range(4):
                        transposes(4 + b, [(ps[:, 4 + b, 256 * e + P * t:256 * e + P * t + P],
                                            memtok[:, t, P * (2 * b + e):P * (2 * b + e) + P])
                                           for e in range(2) for t in range(MT)], m_T)

            for c in range(N_G0):
                n = Slot(c)
                if c in (4, 5, 10, 11):
                    pair_V(n, hH, hL)
                elif c < N_G0 - 1:
                    pair_T(n, hH, hL)
                else:
                    enter(n)
                    vh, vl = weights(n, None, KD, 256)
                    tile_product(n, 0, KD, 256, 0, KD, hH, hL, first_done)
                    for t in range(NT):
                        f = slice(P * t, P * t + P)
                        product(ps[:, 2 * n.s + 1, f], [(hH[:, k, f], hL[:, k, f], vh[:, k, P:2 * P], vl[:, k, P:2 * P])
                                                        for k in range(KD)], slot_done if t == NT - 1 else None)
                job(c)

            def gate_and_branch(n, yh, yl):
                enter(n)
                tile_product(n, 0, 12, P, 0, KD, hH, hL, first_done)
                tile_product(n, 1, 12, P, KD, 12, yh, yl, slot_done, KD)

            for c in range(N_G0, N_LINE):
                if c == N_G0:
                    pe.wait_ge(yc_ready, 1)
                if c == N_G1:
                    pe.wait_ge(ya_ready, 1)
                yh, yl = (ycH, ycL) if c < N_G1 else (yaH, yaL)
                gate_and_branch(Slot(c), yh, yl)
                job(c)
            with pe.Fori(0, (N_G2 - N_LINE) // 2) as i:
                for k in range(2):
                    gate_and_branch(Slot(N_LINE + k, i, 2), yaH, yaL)
            with pe.Fori(0, KD // 2) as i:
                for k in range(2):
                    gate_and_branch(Slot(N_G2 + k, i, 2), ybH, ybL)
            pe.wait_ge(x2_in, 16)
            pe.wait_ge(mix_ready, KD)
            for c in range(4):
                n = Slot(N_OUT + c)
                enter(n)
                vh, vl = weights(n, None, KD, 256)
                for e in range(2):
                    o = ps[:, 2 * n.s + e, :]
                    d0 = P * (2 * c + e)
                    product(o, [(vh[:, k, P * e:P * e + P], vl[:, k, P * e:P * e + P], mixH[:, k, :], mixL[:, k, :])
                                for k in range(KD)], stop=False)
                    for t in range(NT):
                        last = pe.matmul(o[:, P * t:P * t + P], xtok2[:, t, d0:d0 + P], ident[:, :], start=False,
                                         stop=t == NT - 1)
                    last.then_inc((first_done, slot_done)[e], 1)
            pe.wait_ge(m_ready, KD // 2)
            pair_T(Slot(N_MK), memH, memL, width=M)
            pe.wait_ge(x_acc, KD)
            column_sums([[ssqT[:, P * t:P * t + P]] for t in range(NT)], 4, n_ms)
            pair_T(Slot(N_MK + 1), memH, memL, width=M)
            pe.wait_ge(n_rs, 1)
            rows_of(rstd, 5, n_row)
            pe.wait_ge(x_lo, KD)
            pair_T(Slot(N_MQ), hH, hL)
            pair_T(Slot(N_MQ + 1), hH, hL)

            def a_scores(h):
                if h:
                    pe.wait_ge(a_exp, h)
                for t in range(NT):
                    last = pe.matmul(ps[:, 4 + t // 2, 256 * (t % 2):256 * (t % 2) + 256], mq[:, h, P * t:P * t + P],
                                     mkT[:, h, :], start=True, stop=True)
                last.then_inc(a_sc, 1)

            def a_transposes(h):
                pe.wait_ge(a_prob, h + 1)
                if h:
                    pe.wait_ge(a_PT, 2 * h)
                for m in range(MT):
                    transposes(6 + m, [(ps[:, 6 + m, P * t:P * t + P], mP[h % 2][:, t, P * m:P * m + P])
                                       for t in range(NT)], a_T)

            def a_values(h):
                pe.wait_ge(a_PT, 2 * h + 2)
                for m in range(MT):
                    last = pe.matmul(ps[:, h, :], mV[:, m, P * h:P * h + P], mPT[h % 2][:, m, :], start=m == 0,
                                     stop=m == MT - 1)
                last.then_inc(a_o, 1)

            pe.wait_ge(taken, N_MV)
            pe.wait_ge(n_ready, 1)
            a_scores(0)
            pair_V(Slot(N_MV), memH, memL, MT)
            a_scores(1)
            a_transposes(0)
            pair_V(Slot(N_MV + 1), memH, memL, MT)
            a_scores(2)
            a_transposes(1)
            pe.wait_ge(taken, N_MO)
            a_values(0)
            a_scores(3)
            a_transposes(2)
            a_values(1)
            a_transposes(3)
            a_values(2)
            a_values(3)
            pe.wait_ge(a_ready, H)
            with pe.Fori(0, 2) as i:
                for k in range(2):
                    pair_T(Slot(N_MO + k, i, 2), moH, moL, KB)

            pe.wait_ge(x_lo, 2 * KD)

            def up(n):
                enter(n)
                vh, vl = weights(n, None, KD, 256)
                for e, done in ((0, first_done), (1, slot_done)):
                    product(ps[:, 2 * n.s + e, :],
                            [(vh[:, k, P * e:P * e + P], vl[:, k, P * e:P * e + P], hH[:, k, :], hL[:, k, :])
                             for k in range(KD)], done)

            up(Slot(N_UP))
            pe.wait_ge(x_acc, 2 * KD)
            column_sums([[ssqT[:, P * t:P * t + P]] for t in range(NT)], 4, n_ms)
            pe.wait_ge(n_rs, 2)
            rows_of(rstd, 5, n_row)
            up(Slot(N_UP + 1))
            with pe.Fori(0, KF // 2 - 1) as i:
                for k in range(2):
                    up(Slot(N_UP + 2 + k, i, 2))

            def down_half(n, q, half):
                enter(n, banks=False)
                vh, vl = weights(n, None, KH, P)
                product(ps[:, 4 + q, :],
                        [(vh[:, k, :], vl[:, k, :], actH[:, KH * half + k, :], actL[:, KH * half + k, :])
                         for k in range(KH)], slot_done, start=half == 0, stop=half == 1)

            def back(m, q):
                pe.wait_ge(o_g, m.n(1))
                if m.c >= 2:
                    pe.wait_ge(o_tok, m.n(-1))
                transposes(6 + q, [(ps[:, 6 + q, P * t:P * t + P], xg[:, P * t:P * t + P]) for t in range(NT)], o_T)

            def down_tile(m, q):
                n = Slot(N_DN + 2 * m.c, m.i, 2 * m.per)
                if m.c >= 2:
                    pe.wait_ge(o_new, m.n(-1))
                down_half(n, q, 0)
                if m.c >= 1:
                    back(m + -1, 1 - q)
                if m.c == 0:
                    pe.wait_ge(f_ready, KF)
                down_half(n + 1, q, 1)

            pe.wait_ge(f_ready, KH)
            pe.wait_ge(n_ready, 2)
            down_tile(Slot(0), 0)
            down_tile(Slot(1), 1)
            with pe.Fori(0, KD // 2 - 1) as i:
                for q in range(2):
                    down_tile(Slot(2 + q, i, 2), q)
            back(Slot(KD - 1), 1)
            pe.wait_ge(o_acc, KD)
            column_sums([[ssqF[:, P * t:P * t + P]] for t in range(NT)], 0, o_ms)

        @block.scalar
        def _(act):
            q = Order(act, act_step)

            def do(out_ap, in_ap, fn, sem=None, **kw):
                q.sig(act.activation(out_ap, in_ap, fn, **kw), sem)

            def hi(n, width=2048):
                act.wait_ge(raw_in[n.s], n.loads())
                if n.c >= 2:
                    act.wait_ge(slot_done, n.n(-1))
                do(wH[n.s][:, 0:width], raw[n.s][:, 0:width], ACT.Copy, hi_ready)

            act.wait_ge(set_up, 1)
            for t in range(NT):
                act.wait_ge(x_in, 16 * NT)
                if t:
                    q.settle()
                do(junk[:, :], xtok[:, t, :], ACT.Square, accum_out=ssq[:, t:t + 1])
            q.settle()
            do(rstd[:, NT:2 * NT], ssq[:, 0:NT], ACT.Sqrt, std_ready, scale=1.0 / D, bias=eps[:, 0:1])
            act.wait_ge(par_ready, 1)
            for k in range(KD):
                act.wait_ge(xT_out, k + 1)
                do(hH[:, k, :], ps[:, (k + 1) % 8, :], ACT.Copy, h_hi, scale=par[:, G_MIX + k:G_MIX + k + 1])
            hi(Slot(0))
            act.wait_ge(lb_arg, 1)
            do(lbt[:, 1, :], lbt[:, 0, :], ACT.Exp, lb_exp)
            act.wait_ge(ang_ready, 1)
            do(trig[:, 0], ang[:, :, :], ACT.Sin, sin_ready, scale=0.5)
            do(trig[:, 1], ang[:, :, :], ACT.Sin, sin_ready)

            def swaps(dst, src, done):
                for b in range(4):
                    o = 32 * (b ^ 1)
                    do(dst[32 * b:32 * b + 32], src[o:o + 32], ACT.Copy, done)

            def job(n):
                if n == 2:
                    act.wait_ge(taken, 2)
                    do(hgF[:, :, :], hgF[:, :, :], ACT.Sigmoid, hg_sig)
                elif n == 3:
                    act.wait_ge(hg_arg, 2)
                    do(hgF[:, :, :], hgF[:, :, :], ACT.Ln, hg_ln)
                    do(hgl[:, :, :], hgl[:, :, :], ACT.Ln, hg_ln)
                    act.wait_ge(hg_G, H)
                    do(hgK[:, :, :], hgG[:, :, :], ACT.Exp, hg_eG)
                    do(e16[:, :, :], hgG[:, :, :].rearrange("p h (n t) -> p h n t", t=HG_T)[:, :, :, HG_T - 1],
                       ACT.Exp, hg_e16)
                    act.wait_ge(hg_diff, 1)
                    do(hgF[:, :, :], hgF[:, :, :], ACT.Exp, hg_ed)
                elif n == 4:
                    act.wait_ge(taken, 4)
                    do(hgQ[:, :, :], hgQ[:, :, :], ACT.Silu, hg_qs)
                    act.wait_ge(hg_qin, 1)
                    do(hgK[:, :, :], hgG[:, :, :], ACT.Exp, hg_enG, scale=-1.0)
                elif n == 8:
                    act.wait_ge(taken, 8)
                    do(hgO[:, :, :], hgO[:, :, :], ACT.Silu, hg_og)
                elif n == 10:
                    act.wait_ge(taken, 10)
                    swaps(rsw, rqk, r_sw)
                elif n == 12:
                    act.wait_ge(lev_taken, 22)
                    for h in range(H):
                        act.wait_ge(hg_o, h + 1)
                        do(hgY[:, h, :], ps[:, 4 + h, :], ACT.Copy)
                        do(hgsq[:, h, :], ps[:, 4 + h, :], ACT.Square, hg_sq)
                elif n == 13:
                    act.wait_ge(hg_ms, 1)
                    do(stat[:, 0:NT], ps[:, 4, 0:NT], ACT.Sqrt, hg_std, scale=1.0 / (H * P), bias=eps[:, 0:1])
                elif n == 14:
                    act.wait_ge(hg_yf, 1)
                    do(ycH[:, :, :], hgY[:, :, :], ACT.Copy, hg_hi)
                elif n == 15:
                    act.wait_ge(taken, 14)
                    do(rG[:, :, :], rG[:, :, :], ACT.Silu, r_g)
                elif n == 18:
                    for h in range(H):
                        act.wait_ge(r_o, h + 1)
                        do(rY[:, h, :], ps[:, 4 + h, :], ACT.Copy)
                        do(rsq[:, h, :], ps[:, 4 + h, :], ACT.Square, r_sqd)
                    act.wait_ge(taken, 17)
                    swaps(ssw, sq, s_sw)
                    swaps(ssk, sk, s_sw)
                elif n == 19:
                    act.wait_ge(r_ms, 1)
                    do(stat[:, :], ps[:, 4, 0:16], ACT.Sqrt, r_std, scale=1.0 / P, bias=eps[:, 0:1])
                elif n == 20:
                    act.wait_ge(r_yf, 1)
                    do(yaH[:, :, :], rY[:, :, :], ACT.Copy, r_hi)
                    act.wait_ge(s_rope, 1)
                    for v in range(2):
                        for r in range(2):
                            do(kd[64 * r:64 * r + 64, v, :], sk[64 * v:64 * v + 64, :], ACT.Copy)
                    do(vb[0:64, :, :], sv[0:64, :, :], ACT.Copy)
                    do(vb[64:128, 1:NT, :], sv[64:128, 0:NT - 1, :], ACT.Copy, s_kd)
                elif n in (21, 22):
                    hf = n - 21
                    act.wait_ge(s_arg, hf + 1)
                    do(sP[hf][:, :, :], sP[hf][:, :, :], ACT.Exp)
                    do(snk[:, hf, :], snk[:, hf, :], ACT.Exp, s_exp)
                if n in (23, 25):
                    hf = (n - 23) // 2
                    for b in range(4):
                        act.wait_ge(s_T, 4 * hf + b + 1)
                        do(sPT[:, 4 * b:4 * b + 4, :], ps[:, 4 + b, :].rearrange("p (u t) -> p u t", u=4), ACT.Copy,
                           s_PT)
                if n in (24, 26):
                    hf = (n - 24) // 2
                    act.wait_ge(s_o, hf + 1)
                    do(ybH[:, :, 256 * hf:256 * hf + 256], ps[:, 4:6, :].rearrange("p v (a t) -> p (v a) t", a=2),
                       ACT.Copy, s_hi)
                if n == 25:
                    act.wait_ge(mem_in, 16)
                    for t in range(MT):
                        if t:
                            q.settle()
                        do(mjunk[:, :], memtok[:, t, :], ACT.Square, accum_out=memst[:, t:t + 1])
                    q.settle()
                    do(memst[:, 2:4], memst[:, 0:2], ACT.Sqrt, m_std, scale=1.0 / D, bias=eps[:, 0:1])
                    act.wait_ge(m_rs, 1)
                    for t in range(MT):
                        do(memtok[:, t, :], memtok[:, t, :], ACT.Copy, m_norm if t else None,
                           scale=memst[:, 4 + t:5 + t])

            def gate_sigmoid(n):
                act.wait_ge(g_in, n.n(1 - N_G0))
                do(gate[n.s][:, :], gate[n.s][:, :], ACT.Sigmoid, g_sig)

            for c in range(N_LINE):
                hi(Slot(c + 1), 2048 if c + 1 < N_G0 else 12 * P)
                job(c)
                if c >= N_G0:
                    gate_sigmoid(Slot(c))
            for b in range(4):
                act.wait_ge(m_T, b + 1)
                for e in range(2):
                    do(memH[:, 2 * b + e, :], ps[:, 4 + b, 256 * e:256 * e + 256], ACT.Copy, m_hi,
                       scale=par[:, G_MEMN + 2 * b + e:G_MEMN + 2 * b + e + 1])
            turns = (N_G2 - N_LINE) // 2
            with act.Fori(0, turns) as i:
                q.enter(i, [(hi_ready, 2), (g_sig, 2)])
                for k in range(2):
                    n = Slot(N_LINE + k, i, 2)
                    hi(n + 1, 12 * P)
                    gate_sigmoid(n)
                q.leave(turns)

            def mix_upper(n):
                j = n.n(-N_G2)
                act.wait_ge(mix_sum, n.n(1 - N_G2))
                do(mixH[:, bass.ds(j, 1), :], mix[:, bass.ds(j, 1), :], ACT.Copy, mix_hi)

            turns = KD // 2
            with act.Fori(0, turns) as i:
                q.enter(i, [(hi_ready, 2), (g_sig, 2), (mix_hi, 2)])
                for k in range(2):
                    n = Slot(N_G2 + k, i, 2)
                    hi(n + 1, 2048)
                    gate_sigmoid(n)
                    mix_upper(n)
                q.leave(turns)

            def new_x(n, c, e, gain):
                if c == 0:
                    act.wait_ge(x_new, n)
                else:
                    act.wait_ge(taken, n)
                if e.c:
                    act.wait_ge(x_acc, e.n())
                t = xT[:, bass.ds(e.n(0 if gain == G_MEM else -KD), 1), :]
                g = e.n(gain if gain == G_MEM else gain - KD)
                do(hH[:, bass.ds(e.n(0 if gain == G_MEM else -KD), 1), :], t, ACT.Copy, x_hi, scale=par[:, bass.ds(g, 1)])
                do(sqr[:, :], t, ACT.Square, x_sq)

            for c in range(4):
                n = Slot(N_OUT + c)
                hi(n + 1)
                for e in range(2):
                    new_x(n.n(1 - N_OUT) if e == 0 else n.n(1), e, Slot(2 * c + e), G_MEM)
            hi(Slot(N_MK + 1))
            act.wait_ge(n_ms, 1)
            do(rstd[:, NT:2 * NT], ps[:, 4, 0:NT], ACT.Sqrt, n_std, scale=1.0 / D, bias=eps[:, 0:1])
            hi(Slot(N_MQ))
            hi(Slot(N_MQ + 1))
            hi(Slot(N_MV))
            hi(Slot(N_MV + 1))
            scale = float(P) ** -0.5

            def a_exps(h):
                act.wait_ge(a_max, h + 1)
                if h >= 2:
                    act.wait_ge(a_T, 2 * h - 2)
                for t in range(NT):
                    do(mP[h % 2][:, t, :], ps[:, 4 + t // 2, 256 * (t % 2):256 * (t % 2) + 256], ACT.Exp,
                       a_exp if t == NT - 1 else None, scale=scale, bias=mstat[:, 1, h, t:t + 1],
                       accum_out=mstat[:, 2, h, t:t + 1])

            def a_transposed(h):
                for m in range(MT):
                    act.wait_ge(a_T, 2 * h + m + 1)
                    if h >= 2:
                        act.wait_ge(a_o, h - 1)
                    do(mPT[h % 2][:, m, :], ps[:, 6 + m, :], ACT.Copy, a_PT)

            def a_upper(h):
                act.wait_ge(a_o, h + 1)
                do(moH[:, h, :], ps[:, h, :], ACT.Copy, a_hi)

            a_exps(0)
            hi(Slot(N_MO), 4 * 256)
            a_exps(1)
            a_transposed(0)
            a_exps(2)
            a_transposed(1)
            a_upper(0)
            a_exps(3)
            a_transposed(2)
            a_upper(1)
            a_transposed(3)
            a_upper(2)
            a_upper(3)
            with act.Fori(0, 2) as i:
                q.enter(i, [(hi_ready, 2), (x_hi, 4), (x_sq, 4)])
                for k in range(2):
                    n = Slot(N_MO + k, i, 2)
                    hi(n + 1, 2048 if k else 4 * 256)
                    for e in range(2):
                        new_x(n.n(1 - N_MO + 4) if e == 0 else n.n(1), e, Slot(KD + 2 * k + e, i, 4), G_FFN)
                q.leave(2)

            def ffn(n):
                act.wait_ge(f_conv, n.n(1 - N_UP))
                do(ca[:, :], ca[:, :], ACT.Silu, f_silu)
                act.wait_ge(f_prod, n.n(1 - N_UP))
                do(actH[:, bass.ds(n.n(-N_UP), 1), :], prod[:, :], ACT.Copy, f_hi)

            hi(Slot(N_UP + 1))
            act.wait_ge(n_ms, 2)
            do(rstd[:, NT:2 * NT], ps[:, 4, 0:NT], ACT.Sqrt, n_std, scale=1.0 / D, bias=eps[:, 0:1])
            ffn(Slot(N_UP))
            hi(Slot(N_UP + 2))
            ffn(Slot(N_UP + 1))
            turns = KF // 2 - 1
            with act.Fori(0, turns) as i:
                q.enter(i, [(hi_ready, 2), (f_silu, 2), (f_hi, 2)])
                for k in range(2):
                    n = Slot(N_UP + 2 + k, i, 2)
                    hi(n + 1)
                    ffn(n)
                q.leave(turns)

            def result(m, qq):
                act.wait_ge(o_new, m.n(1))
                if m.c:
                    act.wait_ge(o_acc, m.n())
                do(fsq[:, :], xT[:, bass.ds(m.n(), 1), :], ACT.Square, o_sq)

            def to_frames(m, qq):
                act.wait_ge(o_T, m.n(1))
                do(otok[:, :, bass.ds(m.n() * P, P)], ps[:, 6 + qq, :].rearrange("p (t d) -> p t d", t=NT), ACT.Copy,
                   o_tok)

            def down_tile(m, qq):
                n = Slot(N_DN + 2 * m.c, m.i, 2 * m.per)
                hi(n + 1, KH * P)
                if m.c:
                    to_frames(m + -1, 1 - qq)
                if m.c < KD - 1:
                    hi(n + 2, KH * P)
                result(m, qq)

            act.wait_ge(f_ready, KF)
            down_tile(Slot(0), 0)
            down_tile(Slot(1), 1)
            turns = KD // 2 - 2
            with act.Fori(0, turns) as i:
                q.enter(i, [(hi_ready, 4), (o_tok, 2), (o_sq, 2)])
                for k in range(2):
                    down_tile(Slot(2 + k, i, 2), k)
                q.leave(turns)
            down_tile(Slot(KD - 2), 0)
            down_tile(Slot(KD - 1), 1)
            to_frames(Slot(KD - 1), 1)
            act.wait_ge(o_ms, 1)
            do(rstd[:, NT:2 * NT], ps[:, 0, 0:NT], ACT.Sqrt, o_std, scale=1.0 / D, bias=eps[:, 0:1])

        @block.vector
        def _(dve):
            q = Order(dve, dve_step)

            def tt(out_ap, a, b, op, sem=None):
                q.sig(dve.tensor_tensor(out_ap, a, b, op), sem)

            def ts(out_ap, a, s1, s2, op0, op1=None, sem=None):
                q.sig(dve.tensor_scalar(out_ap, a, s1, s2, op0, op1) if op1 is not None
                      else dve.tensor_scalar(out_ap, a, s1, None, op0), sem)

            def stt(out_ap, a, s, b, op0, op1, sem=None):
                q.sig(dve.scalar_tensor_tensor(out_ap, a, s, b, op0, op1), sem)

            def copy(out_ap, a, sem=None):
                q.sig(dve.tensor_copy(out_ap, a), sem)

            def lo(n, width=2048):
                dve.wait_ge(hi_ready, n.n(1))
                tt(wL[n.s][:, 0:width], raw[n.s][:, 0:width], wH[n.s][:, 0:width].bitcast(F32), ALU.subtract, lo_ready)

            q.sig(dve.memset(ones[:, :], 1.0))
            q.sig(dve.memset(restart[:, :], 1.0))
            q.settle()
            q.sig(dve.memset(restart[:, :].rearrange("p (n t) -> p n t", t=HG_T)[:, :, 0:1], 0.0))
            q.sig(dve.memset(eps[:, :], EPS), set_up)
            dve.wait_ge(par_T, 1)
            copy(par[:, :], ps[:, 0, 0:R_ALL], par_ready)
            q.settle()
            logits = par[:, R_HG + H:R_HG + 2 * H]
            tt(lbt[:, 0, :], logits, logits, ALU.subtract, lb_arg)
            dve.wait_ge(std_ready, 1)
            q.sig(dve.reciprocal(rstd[:, 0:NT], rstd[:, NT:2 * NT]), rstd_ready)
            for k in range(KD):
                dve.wait_ge(h_hi, k + 1)
                stt(hL[:, k, :], ps[:, (k + 1) % 8, :], par[:, G_MIX + k:G_MIX + k + 1], hH[:, k, :].bitcast(F32),
                    ALU.mult, ALU.subtract, h_ready)
            lo(Slot(0))
            dve.wait_ge(const_in, 8 * 16)
            copy(posf[:, :], posi[:, :])
            q.settle()
            for t in range(NT):
                ts(ang[:, t, :], invf[:, :], posf[:, t:t + 1], None, ALU.mult)
            parts = split_two_pi()
            for f in (2.0 ** 11, 1.0):
                q.settle()
                ts(turn[:, :, :], ang[:, :, :], 1.0 / (2 * np.pi * f), MAGIC, ALU.mult, ALU.add)
                q.settle()
                ts(turn[:, :, :], turn[:, :, :], MAGIC, None, ALU.subtract)
                for part in parts:
                    q.settle()
                    stt(ang[:, :, :], turn[:, :, :], -part * f, ang[:, :, :], ALU.mult, ALU.add)
            q.settle()
            ts(ang[:, :, :], ang[:, :, :], float(np.float32(3.1415925)), -float(np.float32(3.1415925)), ALU.min,
               ALU.max, ang_ready)
            dve.wait_ge(lb_exp, 1)
            q.sig(dve.reciprocal(lbt[:, 0, :], lbt[:, 1, :]))
            q.settle()
            tt(lbt[:, 0, :], lbt[:, 0, :], lbt[:, 1, :], ALU.mult)
            q.settle()
            tt(lb[:, 0, :], lbt[:, 0, :], lbt[:, 0, :], ALU.subtract)
            q.settle()
            ts(lb[:, 1, :], lb[:, 0, :], -1.0, 1.0, ALU.mult, ALU.add)
            for cp in range(2):
                for cm in range(2):
                    copy(sink16[:, cp, :, cm, :], sinks[:, :, :])

            def read_T(n, dst0, dst1):
                for e, (dst, ready, sem) in enumerate(((dst0, first_done, None), (dst1, slot_done, taken))):
                    dve.wait_ge(ready, n.n(1))
                    tt(dst, ps[:, 2 * n.s + e, :], rstd_row[:, :], ALU.mult, sem)

            def read_V(n, dst, c0):
                for t in range(NT):
                    if t % 2 == 0:
                        dve.wait_ge((first_done, slot_done)[t // 2], n.n(1))
                    ts(dst[:, t, c0:c0 + 256], ps[:, 2 * n.s + t // 2, 256 * (t % 2):256 * (t % 2) + 256],
                       rstd[:, t:t + 1], None, ALU.mult, sem=taken if t == NT - 1 else None)

            def halves(t, size):
                return t[:, :, :].rearrange("p h (n two t) -> p (h n) two t", two=2, t=size)

            def wider(e, size, sem):
                pairs = e[:, :, :].rearrange("p h (n two) -> p (h n) two", two=2)
                n = H * S // (2 * size)
                f, g = halves(hgF, size)[:, :, 0, :], halves(hgQ, size)[:, :, 1, :]
                tt(f, f, pairs[:, :, 1:2].to_broadcast([P, n, size]), ALU.mult)
                tt(g, g, pairs[:, :, 0:1].to_broadcast([P, n, size]), ALU.mult, sem)

            def wide_decay(dst, src):
                v = src[:, :, :].rearrange("p h (n two) -> p h n two", two=2)
                tt(dst[:, :, :], v[:, :, :, 0], v[:, :, :, 1], ALU.mult)

            def level_in(li):
                for i in range(NT):
                    dve.wait_ge(lev_out, 4 * li + i + 1)
                    q.sig(dve.copy_predicated(att[i][:, :, 0:P],
                                              masks[:, li, :].bitcast(U32).unsqueeze(1).to_broadcast([P, H, P]),
                                              ps[:, 4 + i, :].rearrange("p (h t) -> p h t", h=H)), lev_taken)

            def row4(t):
                return t.unsqueeze(1).to_broadcast([P, 4, S])

            def job(n):
                if n == 0:
                    dve.wait_ge(sin_ready, 2)
                    tt(turn[:, :, :], trig[:, 0], trig[:, 0], ALU.mult)
                    q.settle()
                    for b in range(4):
                        ts(wide[:, 0, :, b, :], turn[:, :, :], -2.0, 1.0, ALU.mult, ALU.add)
                        ts(wide[:, 1, :, b, :], trig[:, 1], 1.0 if b % 2 else -1.0, None, ALU.mult,
                           sem=wide_ready if b == 3 else None)
                    dve.wait_ge(row_out, 1)
                    copy(rstd_row[:, :], ps[:, 4, :])
                    q.settle()
                elif n == 1:
                    dve.wait_ge(tab_out, 2)
                    copy(cosT[:, :], ps[:, 5, :], tab_ready)
                    copy(sinT[:, :], ps[:, 6, :], tab_ready)
                elif n == 2:
                    dve.wait_ge(hg_sig, 1)
                    for h in range(H):
                        ts(hgF[:, h, :], hgF[:, h, :], lb[:, 1, h:h + 1], lb[:, 0, h:h + 1], ALU.mult, ALU.add)
                    q.settle()
                    ts(hgk[:, :, :], hgF[:, :, :], -1.0, 1.0, ALU.mult, ALU.add)
                    ts(hgl[:, :, :], hgF[:, :, :], 2.0 ** 60, 1.0, ALU.mult, ALU.min, hg_arg)
                    q.settle()
                    ts(hgF[:, :, :], hgF[:, :, :], 2.0 ** -60, None, ALU.max, sem=hg_arg)
                elif n == 3:
                    dve.wait_ge(hg_ln, 2)
                    tt(hgF[:, :, :], hgF[:, :, :], hgl[:, :, :], ALU.add)
                    q.settle()
                    for h in range(H):
                        q.sig(dve.tensor_tensor_scan(hgG[:, h, :], restart[:, :], hgF[:, h, :], 0.0, ALU.mult,
                                                     ALU.add), hg_G)
                    q.settle()
                    g4 = hgG[:, :, :].rearrange("p h (n t) -> p (h n) t", t=HG_T)
                    tt(hgF[:, :, :].rearrange("p h (n t) -> p (h n) t", t=HG_T),
                       g4[:, :, HG_T - 1:HG_T].to_broadcast([P, H * S // HG_T, HG_T]), g4, ALU.subtract, hg_diff)
                elif n == 4:
                    dve.wait_ge(hg_eG, 1)
                    dve.wait_ge(hg_qs, 1)
                    stt(hgQ[:, :, :], hgQ[:, :, :], float(P) ** -0.5, hgK[:, :, :], ALU.mult, ALU.mult, hg_qin)
                    dve.wait_ge(hg_e16, 1)
                    wide_decay(e32, e16)
                    q.settle()
                    wide_decay(e64, e32)
                    q.settle()
                    wide_decay(e128, e64)
                elif n == 5:
                    dve.wait_ge(hg_enG, 1)
                    tt(hgK[:, :, :], hgK[:, :, :], hgk[:, :, :], ALU.mult, hg_kq)
                    dve.wait_ge(hg_ed, 1)
                    tt(hgF[:, :, :], hgF[:, :, :], hgk[:, :, :], ALU.mult, hg_kq)
                elif n == 6:
                    dve.wait_ge(att_zero, NT)
                    level_in(0)
                elif n == 7:
                    level_in(1)
                    wider(e16, 16, lev_kq)
                elif n == 8:
                    level_in(2)
                    wider(e32, 32, lev_kq)
                elif n == 9:
                    level_in(3)
                    wider(e64, 64, lev_kq)
                elif n == 10:
                    for m, i in enumerate((0, 2)):
                        dve.wait_ge(lev_out, 17 + m)
                        copy(att[i][:, :, P:2 * P], ps[:, 4 + m, :].rearrange("p (h t) -> p h t", h=H), lev_taken)
                    q.settle()
                    f, g = hgF[:, :, 0:P], hgQ[:, :, 3 * P:S]
                    tt(f, f, e128[:, :, 1:2].to_broadcast([P, H, P]), ALU.mult)
                    tt(g, g, e128[:, :, 2:3].to_broadcast([P, H, P]), ALU.mult, lev_kq)
                elif n == 11:
                    for m in range(4):
                        dve.wait_ge(lev_out, 19 + m)
                        i, h0 = m // 2, 2 * (m % 2)
                        copy(att[i][:, h0:h0 + 2, 2 * P - P * i:S - P * i],
                             ps[:, 4 + m, :].rearrange("p (h t) -> p h t", h=2), lev_taken)
                    dve.wait_ge(r_sw, 4)
                    dve.wait_ge(tab_ready, 2)
                    tt(rsw[:, :, :], rsw[:, :, :], row4(sinT[:, :]), ALU.mult)
                elif n == 12:
                    tt(rqk[:, :, :], rqk[:, :, :], row4(cosT[:, :]), ALU.mult)
                    q.settle()
                    tt(rqk[:, :, :], rqk[:, :, :], rsw[:, :, :], ALU.add, r_rope)
                elif n == 13:
                    dve.wait_ge(hg_std, 1)
                    q.sig(dve.reciprocal(statr[:, 0:NT], stat[:, 0:NT]), hg_rs)
                    dve.wait_ge(hg_og, 1)
                    dve.wait_ge(hg_sq, H)
                    for h in range(H):
                        stt(hgY[:, h, :], hgY[:, h, :], par[:, R_HG + h:R_HG + h + 1], hgO[:, h, :], ALU.mult, ALU.mult)
                elif n == 14:
                    dve.wait_ge(hg_row, 1)
                    q.settle()
                    tt(hgY[:, :, :], hgY[:, :, :], row4(ps[:, 4, :]), ALU.mult, hg_yf)
                elif n == 15:
                    dve.wait_ge(hg_hi, 1)
                    tt(ycL[:, :, :], hgY[:, :, :], ycH[:, :, :].bitcast(F32), ALU.subtract, yc_ready)
                    for h in range(H):
                        dve.wait_ge(r_sc, h + 1)
                        tt(att[0][:, h, :], ps[:, 4 + h, :], decay[:, h, :], ALU.mult, r_att)
                elif n == 16:
                    for h in range(H):
                        dve.wait_ge(r_sc, H + h + 1)
                        tt(att[1][:, h, :], ps[:, 4 + h, 0:S - P], decay[:, h, 0:S - P], ALU.mult, r_att)
                elif n == 17:
                    for m, (i, r) in enumerate(((2, 0), (2, 1), (3, 0), (3, 1))):
                        w = S - P * i
                        dve.wait_ge(r_sc, 2 * H + m + 1)
                        tt(att[i][:, :, :].rearrange("p (v r) t -> p r v t", r=2)[:, r],
                           ps[:, 4 + m, :].rearrange("p (v t) -> p v t", v=2)[:, :, 0:w],
                           decay[:, :, 0:w].rearrange("p (v r) t -> p r v t", r=2)[:, r], ALU.mult, r_att)
                    q.settle()
                elif n == 18:
                    dve.wait_ge(s_sw, 8)
                    tt(ssw[:, :, :], ssw[:, :, :], row4(sinT[:, :]), ALU.mult)
                    tt(ssk[:, :], ssk[:, :], sinT[:, :], ALU.mult)
                elif n == 19:
                    dve.wait_ge(r_std, 1)
                    q.sig(dve.reciprocal(statr[:, :], stat[:, :]), r_rs)
                    dve.wait_ge(r_g, 1)
                    dve.wait_ge(r_sqd, H)
                    tt(rY[:, :, :], rY[:, :, :], rG[:, :, :], ALU.mult)
                    tt(sq[:, :, :], sq[:, :, :], row4(cosT[:, :]), ALU.mult)
                    tt(sk[:, :], sk[:, :], cosT[:, :], ALU.mult)
                elif n == 20:
                    dve.wait_ge(r_row, 4)
                    q.settle()
                    tt(rY[:, :, :], rY[:, :, :], ps[:, 4:8, :], ALU.mult, r_yf)
                    for v in range(2):
                        a, b = (t[:, 2 * v:2 * v + 2, :].rearrange("p a (c t) -> p a c t", t=L) for t in (sq, ssw))
                        tt(sqc[:, v].rearrange("p c a t -> p a c t"), a, b, ALU.add)
                    tt(sk[:, :], sk[:, :], ssk[:, :], ALU.add, s_rope)
                elif n == 21:
                    dve.wait_ge(r_hi, 1)
                    tt(yaL[:, :, :], rY[:, :, :], yaH[:, :, :].bitcast(F32), ALU.subtract, ya_ready)
                    softmax_in(0)
                elif n == 22:
                    softmax_out(0)
                    softmax_in(1)
                elif n == 23:
                    softmax_out(1)
                elif n in (24, 26):
                    hf = (n - 24) // 2
                    dve.wait_ge(s_hi, hf + 1)
                    f = slice(256 * hf, 256 * hf + 256)
                    tt(ybL[:, :, f], ps[:, 4:6, :].rearrange("p v (a t) -> p (v a) t", a=2), ybH[:, :, f].bitcast(F32),
                       ALU.subtract, yb_ready)
                elif n == 25:
                    dve.wait_ge(m_std, 1)
                    q.sig(dve.reciprocal(memst[:, 4:6], memst[:, 2:4]), m_rs)

            def softmax_in(hf):
                dve.wait_ge(s_sc, hf + 1)
                scores = ps[:, 4:8, :].rearrange("p b (u t) -> p (b u) t", u=4)
                q.sig(dve.reduce_max(smx[:, hf, :], scores, AX_X))
                q.settle()
                s16 = sink16[:, :, :, :, :].rearrange("p a b c d -> p (a b c d)")
                stt(smx[:, hf, :], smx[:, hf, :], float(L) ** -0.5, s16, ALU.mult, ALU.max)
                q.settle()
                tt(snk[:, hf, :], s16, smx[:, hf, :], ALU.subtract)
                stt(sP[hf][:, :, :], scores, float(L) ** -0.5, smx[:, hf, :].unsqueeze(2).to_broadcast([P, 16, P]),
                    ALU.mult, ALU.subtract, s_arg)

            def softmax_out(hf):
                dve.wait_ge(s_exp, hf + 1)
                if hf == 0:
                    for r in range(2):
                        q.sig(dve.memset(sP[0][:, 4 * r:4 * r + 2, L:2 * L], 0.0))
                    q.settle()
                q.sig(dve.reduce_sum(ssum[:, hf, :], sP[hf][:, :, :], AX_X))
                q.settle()
                tt(ssum[:, hf, :], ssum[:, hf, :], snk[:, hf, :], ALU.add)
                q.settle()
                q.sig(dve.reciprocal(ssum[:, hf, :], ssum[:, hf, :]))
                q.settle()
                tt(sP[hf][:, :, :], sP[hf][:, :, :], ssum[:, hf, :].unsqueeze(2).to_broadcast([P, 16, P]), ALU.mult,
                   s_prob)

            def gate_in(n):
                dve.wait_ge(first_done, n.n(1))
                tt(gate[n.s][:, :], ps[:, 2 * n.s, :], rstd_row[:, :], ALU.mult, g_in)

            def gate_out(n, dst, sem=taken):
                dve.wait_ge(slot_done, n.n(1))
                dve.wait_ge(g_sig, n.n(1 - N_G0))
                tt(dst, gate[n.s][:, :], ps[:, 2 * n.s + 1, :], ALU.mult, sem)

            pairs = {0: (hgF, 0), 1: (hgF, 2), 2: (hgQ, 0), 3: (hgQ, 2), 6: (hgO, 0), 7: (hgO, 2), 8: (rqk, 0),
                     9: (rqk, 2), 12: (rG, 0), 13: (rG, 2), 14: (sq, 0), 15: (sq, 2)}
            for c in range(N_G0):
                n = Slot(c)
                lo(n + 1, 2048 if c + 1 < N_G0 else 12 * P)
                job(c)
                if c in pairs:
                    t, e = pairs[c]
                    read_T(n, t[:, e, :], t[:, e + 1, :])
                elif c in (4, 5):
                    read_V(n, hgV, 256 * (c - 4))
                elif c in (10, 11):
                    read_V(n, rV, 256 * (c - 10))
                else:
                    dve.wait_ge(first_done, n.n(1))
                    tt(sk[:, :], ps[:, 2 * n.s, :], rstd_row[:, :], ALU.mult)
                    dve.wait_ge(slot_done, n.n(1))
                    for t in range(NT):
                        ts(sv[:, t, :], ps[:, 2 * n.s + 1, P * t:P * t + P], rstd[:, t:t + 1], None, ALU.mult,
                           sem=taken if t == NT - 1 else None)
            for c in range(N_G0, N_LINE):
                n = Slot(c)
                lo(n + 1, 12 * P)
                job(c)
                gate_in(n)
                if c < N_G1:
                    gate_out(n, mix[:, c - N_G0, :])
                else:
                    gate_out(n, gmix[:, :])
                    q.settle()
                    tt(mix[:, c - N_G1, :], mix[:, c - N_G1, :], gmix[:, :], ALU.add)
            for k in range(KD):
                dve.wait_ge(m_hi, k + 1)
                if k % 2 == 1:
                    for e in (k - 1, k):
                        stt(memL[:, e, :], ps[:, 4 + e // 2, 256 * (e % 2):256 * (e % 2) + 256],
                            par[:, G_MEMN + e:G_MEMN + e + 1], memH[:, e, :].bitcast(F32), ALU.mult, ALU.subtract,
                            m_ready if e == k else None)
            turns = (N_G2 - N_LINE) // 2
            with dve.Fori(0, turns) as i:
                q.enter(i, [(lo_ready, 2), (g_in, 2), (taken, 2), (dve_step, 2)])
                for k in range(2):
                    n = Slot(N_LINE + k, i, 2)
                    lo(n + 1, 12 * P)
                    gate_in(n)
                    gate_out(n, gmix[:, :])
                    q.settle()
                    t = mix[:, bass.ds(n.n(-N_G1), 1), :]
                    tt(t, t, gmix[:, :], ALU.add)
                q.leave(turns)
            turns = KD // 2
            with dve.Fori(0, turns) as i:
                q.enter(i, [(lo_ready, 2), (g_in, 2), (taken, 2), (mix_sum, 2), (mix_ready, 2)])
                for k in range(2):
                    n = Slot(N_G2 + k, i, 2)
                    lo(n + 1, 2048)
                    gate_in(n)
                    gate_out(n, gmix[:, :])
                    q.settle()
                    j = n.n(-N_G2)
                    t = mix[:, bass.ds(j, 1), :]
                    tt(t, t, gmix[:, :], ALU.add, mix_sum)
                    dve.wait_ge(mix_hi, n.n(1 - N_G2))
                    tt(mixL[:, bass.ds(j, 1), :], t, mixH[:, bass.ds(j, 1), :].bitcast(F32), ALU.subtract, mix_ready)
                q.leave(turns)

            def new_x(n, c, e, gain):
                j = e.n(0 if gain == G_MEM else -KD)
                t = xT[:, bass.ds(j, 1), :]
                dve.wait_ge((first_done, slot_done)[c], n.n(1))
                if gain == G_MEM:
                    copy(t, ps[:, 2 * n.s + c, :], (x_new, taken)[c])
                else:
                    tt(t, t, ps[:, 2 * n.s + c, :], ALU.add, (x_new, taken)[c])
                q.settle()
                g = e.n(gain if gain == G_MEM else gain - KD)
                dve.wait_ge(x_hi, e.n(1))
                stt(hL[:, bass.ds(j, 1), :], t, par[:, bass.ds(g, 1)], hH[:, bass.ds(j, 1), :].bitcast(F32), ALU.mult,
                    ALU.subtract, x_lo)
                dve.wait_ge(x_sq, e.n(1))
                tt(ssqT[:, :], ssqT[:, :], sqr[:, :], ALU.add, x_acc)

            def norm_columns(k, last):
                dve.wait_ge(n_std, k)
                q.sig(dve.reciprocal(rstd[:, 0:NT], rstd[:, NT:2 * NT]), n_rs)
                if last:
                    return

            def norm_row(k):
                dve.wait_ge(n_row, k)
                copy(rstd_row[:, :], ps[:, 5, :], n_ready)
                q.settle()

            q.sig(dve.memset(ssqT[:, :], 0.0))
            q.settle()
            for c in range(4):
                n = Slot(N_OUT + c)
                lo(n + 1)
                for e in range(2):
                    new_x(n, e, Slot(2 * c + e), G_MEM)

            def read_keys(n, h):
                for e in range(2):
                    dve.wait_ge((first_done, slot_done)[e], n.n(1))
                    copy(mkT[:, h + e, :], ps[:, 2 * n.s + e, 0:M], taken if e else None)

            def read_values(n, c0):
                for t in range(MT):
                    dve.wait_ge((first_done, slot_done)[t], n.n(1))
                    copy(mV[:, t, c0:c0 + 256], ps[:, 2 * n.s + t, 0:256], taken if t else None)

            def a_maximum(h):
                dve.wait_ge(a_sc, h + 1)
                q.sig(dve.reduce_max(mstat[:, 0, h, :], ps[:, 4:6, :].rearrange("p b (t m) -> p (b t) m", t=2), AX_X))
                q.settle()
                ts(mstat[:, 1, h, :], mstat[:, 0, h, :], -float(P) ** -0.5, None, ALU.mult, sem=a_max)

            def a_normed(h):
                dve.wait_ge(a_exp, h + 1)
                q.sig(dve.reciprocal(mstat[:, 3, h, :], mstat[:, 2, h, :]))
                q.settle()
                tt(mP[h % 2][:, :, :], mP[h % 2][:, :, :], mstat[:, 3, h, :].unsqueeze(2).to_broadcast([P, NT, M]),
                   ALU.mult, a_prob)

            def a_lower(h):
                dve.wait_ge(a_hi, h + 1)
                tt(moL[:, h, :], ps[:, h, :], moH[:, h, :].bitcast(F32), ALU.subtract, a_ready)

            lo(Slot(N_MK + 1))
            norm_columns(1, False)
            read_keys(Slot(N_MK), 0)
            lo(Slot(N_MQ))
            read_keys(Slot(N_MK + 1), 2)
            norm_row(1)
            lo(Slot(N_MQ + 1))
            read_T(Slot(N_MQ), mq[:, 0, :], mq[:, 1, :])
            lo(Slot(N_MV))
            read_T(Slot(N_MQ + 1), mq[:, 2, :], mq[:, 3, :])
            lo(Slot(N_MV + 1))
            a_maximum(0)
            read_values(Slot(N_MV), 0)
            a_normed(0)
            lo(Slot(N_MO), 4 * 256)
            a_maximum(1)
            read_values(Slot(N_MV + 1), 256)
            a_normed(1)
            a_maximum(2)
            a_normed(2)
            a_lower(0)
            a_maximum(3)
            a_normed(3)
            a_lower(1)
            a_lower(2)
            a_lower(3)
            q.sig(dve.memset(ssqT[:, :], 0.0))
            q.settle()
            with dve.Fori(0, 2) as i:
                q.enter(i, [(lo_ready, 2), (x_new, 2), (taken, 2), (x_lo, 4), (x_acc, 4)])
                for k in range(2):
                    n = Slot(N_MO + k, i, 2)
                    lo(n + 1, 2048 if k else 4 * 256)
                    for e in range(2):
                        new_x(n, e, Slot(KD + 2 * k + e, i, 4), G_FFN)
                q.leave(2)

            def conv(n, e):
                z, c = (za, ca) if e == 0 else (zu, cu)
                dve.wait_ge((first_done, slot_done)[e], n.n(1))
                tt(z[:, 2:S + 2], ps[:, 2 * n.s + e, :], rstd_row[:, :], ALU.mult, taken if e else None)
                q.settle()

                def tap(j):
                    return par[:, bass.ds(n.n(R_CONV + 2 * KF * j + KF * e - N_UP), 1)]

                ts(c[:, :], z[:, 2:S + 2], tap(2), tap(3), ALU.mult, ALU.add)
                q.settle()
                stt(c[:, :], z[:, 1:S + 1], tap(1), c[:, :], ALU.mult, ALU.add)
                q.settle()
                stt(c[:, :], z[:, 0:S], tap(0), c[:, :], ALU.mult, ALU.add, f_conv if e == 0 else None)

            def ffn(n):
                conv(n, 0)
                conv(n, 1)
                dve.wait_ge(f_silu, n.n(1 - N_UP))
                q.settle()
                tt(prod[:, :], ca[:, :], cu[:, :], ALU.mult, f_prod)

            def ffn_lower(n):
                dve.wait_ge(f_hi, n.n(1 - N_UP))
                j = bass.ds(n.n(-N_UP), 1)
                tt(actL[:, j, :], prod[:, :], actH[:, j, :].bitcast(F32), ALU.subtract, f_ready)

            q.sig(dve.memset(za[:, 0:2], 0.0))
            q.sig(dve.memset(zu[:, 0:2], 0.0))
            lo(Slot(N_UP + 1))
            norm_columns(2, False)
            norm_row(2)
            ffn(Slot(N_UP))
            lo(Slot(N_UP + 2))
            ffn_lower(Slot(N_UP))
            ffn(Slot(N_UP + 1))
            turns = KF // 2 - 1
            with dve.Fori(0, turns) as i:
                q.enter(i, [(lo_ready, 2), (taken, 2), (f_conv, 2), (f_prod, 2), (f_ready, 2), (dve_step, 12)])
                for k in range(2):
                    n = Slot(N_UP + 2 + k, i, 2)
                    lo(n + 1)
                    ffn_lower(n + -1)
                    ffn(n)
                q.leave(turns)

            def down_tile(m, qq):
                n = Slot(N_DN + 2 * m.c, m.i, 2 * m.per)
                lo(n + 1, KH * P)
                if m.c < KD - 1:
                    lo(n + 2, KH * P)
                j = m.n()
                t = xT[:, bass.ds(j, 1), :]
                dve.wait_ge(slot_done, n.n(2))
                tt(t, t, ps[:, 4 + qq, :], ALU.add, o_new)
                if m.c:
                    dve.wait_ge(o_T, m.n())
                q.settle()
                ts(xg[:, :], t, par[:, bass.ds(m.n(G_FIN), 1)], None, ALU.mult, sem=o_g)
                dve.wait_ge(o_sq, m.n(1))
                tt(ssqF[:, :], ssqF[:, :], fsq[:, :], ALU.add, o_acc)

            ffn_lower(Slot(N_DN - 1))
            q.sig(dve.memset(ssqF[:, :], 0.0))
            q.settle()
            down_tile(Slot(0), 0)
            down_tile(Slot(1), 1)
            turns = KD // 2 - 2
            with dve.Fori(0, turns) as i:
                q.enter(i, [(lo_ready, 4), (o_new, 2), (o_g, 2), (o_acc, 2)])
                for k in range(2):
                    down_tile(Slot(2 + k, i, 2), k)
                q.leave(turns)
            down_tile(Slot(KD - 2), 0)
            down_tile(Slot(KD - 1), 1)
            dve.wait_ge(o_std, 1)
            q.sig(dve.reciprocal(rstd[:, 0:NT], rstd[:, NT:2 * NT]))
            q.settle()
            dve.wait_ge(o_tok, KD)
            for t in range(NT):
                ts(otok[:, t, :], otok[:, t, :], rstd[:, t:t + 1], None, ALU.mult, sem=o_fin)


_INS = ["x", "mem", "positions", "norm_mix_g", "w_in", "swa_sinks", "hg_lb_logits", "hg_norm_g", "w_branch", "w_out",
        "norm_mem_g", "mem_norm_g", "w_mq", "w_mkv", "w_mo", "norm_ffn_g", "w_up", "conv_w", "conv_b", "w_down",
        "final_norm_g"]


def shape_constants():
    c = np.zeros((P, K_ALL), np.float32)
    c[:, K_ID:K_ID + P] = np.eye(P)
    s, t = np.arange(P)[:, None], np.arange(P)[None, :]
    c[:, K_MASK:K_MASK + P] = (s // HG_T == t // HG_T) & (t >= s)
    for i, size in enumerate((16, 32, 64)):
        c[:, K_MASK + P * (i + 1):K_MASK + P * (i + 2)] = (s // size % 2 == 0) & (t // size == s // size + 1)
    j, p = np.arange(S)[None, :], np.arange(P)[:, None]
    for h in range(H):
        log_gamma = np.log1p(-(2.0 ** (-5 - h)))
        c[:, K_DECAY + S * h:K_DECAY + S * (h + 1)] = np.where(j >= p, np.exp(log_gamma * np.maximum(j - p, 0)), 0) / 8
    f = np.float32
    c[:, K_INV:K_INV + 32] = f(1.0) / (f(10000.0) ** (np.arange(0, 64, 2, dtype=f) / f(64)))
    return c


def kernel(**inputs):
    import concourse.bacc as _bacc
    from concourse.bass_utils import run_bass_kernel_spmd as _run

    nc = _bacc.Bacc("TRN2", target_bir_lowering=False, num_devices=1)
    arrays, args = {}, []
    for name, a in [(name, inputs[name]) for name in _INS] + [("consts", shape_constants())]:
        a = np.ascontiguousarray(a)
        arrays[f"in_{name}"] = a
        args.append(nc.dram_tensor(f"in_{name}", a.shape, mybir.dt.from_np(a.dtype), kind="ExternalInput").ap())
    args.append(nc.dram_tensor("out", (1, S, D), F32, kind="ExternalOutput").ap())
    hybrid_layer(nc, *args)
    r = _run(nc, [arrays], core_ids=[0])
    return r.results[0]["out"]
```

```python
from contextlib import ExitStack

import numpy as np

import concourse.bass as bass
from concourse import mybir

ALU = mybir.AluOpType
ACT = mybir.ActivationFunctionType
F32 = mybir.dt.float32
F32R = mybir.dt.float32r
I32 = mybir.dt.int32
U32 = mybir.dt.uint32
AX_X = mybir.AxisListType.X

P = 128
D = 1024
S = 512
KD = D // P
NT = S // P
EPS = 1e-6
L = 64
BR = 512
KB = BR // P
FF = 2816
KF = FF // P
M = 256
MT = M // P
H = 4
HG_T = 16

C_RQ, C_RK, C_RV, C_RG = 0, 256, 512, 1024
C_SQ, C_SK = 1536, 2048
C_HQ, C_HF, C_HI, C_HO = 2304, 2816, 3328, 3840
C_GATE = 4352

PAIRS = [C_HF, C_HF + 256, C_HQ, C_HQ + 256, C_HI, C_HI + 256, C_HO, C_HO + 256,
         C_RQ, C_RK, C_RV, C_RV + 256, C_RG, C_RG + 256, C_SQ, C_SQ + 256, C_SK]
N_G0 = len(PAIRS)
N_G1 = N_G0 + KD
N_LINE = N_G1 + 2
N_G2 = N_G1 + KD
N_OUT = N_G2 + KD
N_MK = N_OUT + 4
N_MQ = N_MK + 1
N_MV = N_MK + 4
N_MO = N_MV + 2
N_UP = N_MO + 4
N_DN = N_UP + KF
KH = KF // 2

K_ID = 0
K_MASK = K_ID + P
K_DECAY = K_MASK + 4 * P
K_INV = K_DECAY + H * S
K_ALL = K_INV + 32

R_CONV = 0
R_GAIN = 4 * 2 * KF
R_HG = R_GAIN + 5 * KD
R_ALL = R_HG + 2 * H
G_MIX, G_MEM, G_MEMN, G_FFN, G_FIN = (R_GAIN + KD * i for i in range(5))

MAGIC = 12582912.0


def split_two_pi():
    parts, rest = [], 2 * np.pi
    for i in range(4):
        scale = 2.0 ** (9 + 12 * i)
        parts.append(float(np.round(rest * scale) / scale))
        rest -= parts[-1]
    return parts


class Slot:

    def __init__(self, c, i=None, per=0):
        self.c, self.i, self.per = c, i, per
        self.s = c % 2

    def __add__(self, k):
        return Slot(self.c + k, self.i, self.per)

    def n(self, k=0):
        return self.c + k if self.i is None else self.i * self.per + (self.c + k)

    def loads(self):
        c = 32 * (self.c // 2 + self.s)
        return c if self.i is None else self.i * (16 * self.per) + c


class Order:

    def __init__(self, eng, own):
        self.eng, self.own, self.count, self.i, self.per = eng, own, {}, None, {}

    def sig(self, ins, sem=None):
        sem = self.own if sem is None else sem
        ins.then_inc(sem, 1)
        self.last = sem
        self.count[sem.name] = self.count.get(sem.name, 0) + 1

    def settle(self):
        n = self.count[self.last.name]
        per = self.per.get(self.last.name, 0)
        self.eng.wait_ge(self.last, n if self.i is None or not per else self.i * per + n)

    def enter(self, i, per):
        self.i, self.per, self.base = i, {s.name: k for s, k in per}, dict(self.count)

    def leave(self, turns):
        for name, n in self.count.items():
            k = n - self.base.get(name, 0)
            assert k == self.per.get(name, 0), (name, k)
            self.count[name] = n + k * (turns - 1)
        self.i, self.per = None, {}


def hybrid_layer(nc, x, mem, positions, norm_mix_g, w_in, swa_sinks, hg_lb_logits, hg_norm_g, w_branch,
                 w_out, norm_mem_g, mem_norm_g, w_mq, w_mkv, w_mo, norm_ffn_g, w_up, conv_w, conv_b,
                 w_down, final_norm_g, consts, out):
    ctx = ExitStack()
    with ctx:
        KIB = 1024
        base = [(nc.sbuf_base + 63) // 64 * 64]

        def at(name, offset, shape, dt=F32):
            return nc.alloc_sbuf_tensor_at(name, shape, dt, offset=offset)

        def fixed(name, shape, dt=F32):
            t = at(name, base[0], shape, dt)
            base[0] += (int(np.prod(shape[1:])) * 4 + 31) // 32 * 32
            return t

        H_AT = base[0]
        hH = fixed("hH", [P, KD, S], F32R)
        hL = fixed("hL", [P, KD, S], F32R)
        raw = [fixed(f"raw{s}", [P, 2048]) for s in range(2)]
        wH = [fixed(f"wH{s}", [P, 2048], F32R) for s in range(2)]
        wL = [fixed(f"wL{s}", [P, 2048], F32R) for s in range(2)]
        ident = fixed("ident", [P, P])
        ones = fixed("ones", [P, 8])
        par = fixed("par", [P, R_ALL])
        rstd_row = fixed("rstd_row", [P, S])
        rstd = fixed("rstd", [P, 2 * NT])
        eps = fixed("eps", [P, 8])
        ssq = fixed("ssq", [P, 8])
        U0 = base[0]
        A = U0 + 16 * KIB
        U = [U0, U0 + 8 * KIB] + [A + 8 * KIB * i for i in range(6)]
        U_AT = A + 48 * KIB
        U_R = U_AT + 20 * KIB
        U_C = U_R + 16 * KIB

        masks = at("masks", U_C, [P, 4, P])
        decay = at("decay", U_C + 2 * KIB, [P, H, S])
        cosT = at("cosT", U_C + 10 * KIB, [P, S])
        sinT = at("sinT", U_C + 12 * KIB, [P, S])
        sv = at("sv", U_C + 14 * KIB, [P, NT, P])
        sk = at("sk", U_C + 16 * KIB, [P, S])
        svT = at("svT", U_C + 6 * KIB, [P, S])
        restart = at("restart", U_C + 16 * KIB, [P, S])
        T = U_C + 18 * KIB
        e16 = at("e16", T, [P, H, 32])
        e32 = at("e32", T + 512, [P, H, 16])
        e64 = at("e64", T + 768, [P, H, 8])
        e128 = at("e128", T + 896, [P, H, 4])
        lb = at("lb", T + 960, [P, 2, H])
        lbt = at("lbt", T + 992, [P, 2, H])
        stat = at("stat", T + 1024, [P, 16])
        statr = at("statr", T + 1088, [P, 16])
        sinks = at("sinks", T + 1152, [P, 2, 2])
        sink16 = at("sink16", T + 1184, [P, 2, 2, 2, 2])
        smx = at("smx", T + 1248, [P, 2, 16])
        snk = at("snk", T + 1376, [P, 2, 16])
        ssum = at("ssum", T + 1504, [P, 2, 16])
        invf = at("invf", T + 1632, [P, 32])
        mstat = at("mstat", T + 1760, [P, 4, H, NT])
        memst = at("memst", T + 2016, [P, 8])
        assert T + 2048 <= nc.sbuf_usable_end

        xtok = at("xtok", U_R, [P, NT, D])
        junk = at("junk", U[0], [P, D])
        rows_conv = at("rows_conv", U[2], [2 * KF, 4, P])
        rows_gain = at("rows_gain", U[2] + 2 * KIB, [KD, 5, P])
        rows_hg = at("rows_hg", U[2] + 5 * KIB, [H, 2, P])
        posi = at("posi", U[3], [P, NT], I32)
        posf = at("posf", U[3] + 32, [P, NT])
        ang = at("ang", U[3] + 1024, [P, NT, 32])
        whole = [at(f"whole{i}", U[3] + o, [P, NT, 32]) for i, o in enumerate((1536, 3072, 3584))]
        trig = at("trig", U[3] + 2048, [P, 2, NT, 32])
        wide = at("wide", U[3] + 4096, [P, 2, NT, 4, 32])

        hgF = at("hgF", U[0], [P, H, S])
        hgQ = at("hgQ", U[1], [P, H, S])
        hgK = at("hgK", U[2], [P, H, S])
        hgG = at("hgG", U[3], [P, H, S])
        hgk = at("hgk", U[4], [P, H, S])
        hgl = at("hgl", U_R, [P, H, S])
        hgO = at("hgO", U[5], [P, H, S])
        hgV = at("hgV", U[6], [P, NT, BR])
        hgY = at("hgY", U[1], [P, H, S])
        hgsq = at("hgsq", U[0], [P, H, S])
        att = [at(f"att{i}", U_AT + o * KIB, [P, H, S - P * i]) for i, o in enumerate((0, 8, 14, 18))]
        ycH = at("ycH", U_R, [P, KB, S], F32R)
        ycL = at("ycL", U_R + 8 * KIB, [P, KB, S], F32R)
        rqk = at("rqk", U[2], [P, 4, S])
        rsw = at("rsw", U[4], [P, 4, S])
        rV = at("rV", U[3], [P, NT, BR])
        rG = at("rG", U[7], [P, H, S])
        rY = at("rY", U[4], [P, H, S])
        rsq = at("rsq", U[2], [P, H, S])
        yaH = at("yaH", U[2], [P, KB, S], F32R)
        yaL = at("yaL", U[3], [P, KB, S], F32R)
        sq = at("sq", U[6], [P, 4, S])
        sqc = at("sqc", U_AT, [P, 2, S // L, 2, L])
        ssw = at("ssw", U[5], [P, 4, S])
        ssk = at("ssk", U_C + 8 * KIB, [P, S])
        kd = at("kd", U_AT + 12 * KIB, [P, 2, S])
        vb = at("vb", U_AT + 16 * KIB, [P, NT, P])
        sP = [at("sP0", U[7], [P, 16, P]), at("sP1", U_AT, [P, 16, P])]
        sPT = at("sPT", U[6], [P, 16, P])
        ybH = at("ybH", U[5], [P, KB, S], F32R)
        ybL = at("ybL", U[7], [P, KB, S], F32R)
        mix = at("mix", U0, [P, KD, S])
        mixH = at("mixH", U[2], [P, KD, S], F32R)
        mixL = at("mixL", U_AT, [P, KD, S], F32R)
        gate = [at(f"gate{s}", U_C + (2 + 2 * s) * KIB, [P, S]) for s in range(2)]
        gmix = at("gmix", U_C + 6 * KIB, [P, S])
        xT = at("xT", U0, [P, KD, S])
        xtok2 = at("xtok2", U_R, [P, NT, D])
        sqr = at("sqr", U_C + 8 * KIB, [P, S])
        ssqT = at("ssqT", U[4] + 4 * KIB, [P, S])
        memtok = at("memtok", U[4], [P, MT, D])
        mjunk = at("mjunk", U_AT + 8 * KIB, [P, D])
        memH = at("memH", U_C + 10 * KIB, [P, KD, M], F32R)
        memL = at("memL", U[6], [P, KD, M], F32R)
        mkT = at("mkT", U_AT + 16 * KIB, [P, H, M])
        mV = at("mV", U[4], [P, MT, BR])
        mq = at("mq", U[5], [P, H, S])
        mP = [at(f"mP{i}", U[7] + 4 * KIB * i, [P, NT, M]) for i in range(2)]
        mPT = [at(f"mPT{i}", U[2] + 4 * KIB * i, [P, MT, S]) for i in range(2)]
        moH = at("moH", U[3], [P, H, S], F32R)
        moL = at("moL", U_AT, [P, H, S], F32R)
        actH = at("actH", A, [P, KF, S], F32R)
        actL = at("actL", A + 44 * KIB, [P, KF, S], F32R)
        B = A + 88 * KIB
        za = at("za", B, [P, S + 2])
        zu = at("zu", B + 2080, [P, S + 2])
        ca = at("ca", B + 4160, [P, S])
        cu = at("cu", B + 4160 + 2 * KIB, [P, S])
        prod = at("prod", B + 4160 + 4 * KIB, [P, S])
        fsq = at("fsq", B + 4160 + 6 * KIB, [P, S])
        xg = at("xg", B + 4160 + 8 * KIB, [P, S])
        ssqF = at("ssqF", B + 4160 + 10 * KIB, [P, S])
        assert B + 4160 + 12 * KIB <= nc.sbuf_usable_end
        otok = at("otok", H_AT, [P, NT, D])

        ps = ctx.enter_context(nc.psum_tensor("ps", [P, 8, S], F32))

        def sems(names):
            return [ctx.enter_context(nc.semaphore(name)) for name in names.split()]

        raw_in = sems("raw_in0 raw_in1")
        x_in = sems("x_in0 x_in1 x_in2 x_in3")
        ident_in, const_in, par_in, mem_in, x2_in, out_done = sems(
            "ident_in const_in par_in mem_in x2_in out_done")
        hi_ready, lo_ready, first_done, slot_done, taken = sems("hi_ready lo_ready first_done slot_done taken")
        first_in = sems("first_in0 first_in1")
        first_half, half_ready = sems("first_half half_ready")
        dve_step, act_step = sems("dve_step act_step")
        (set_up, att_zero, par_T, par_ready, std_ready, rstd_ready, xT_out, h_hi, h_ready, row_out, lb_arg,
         lb_exp, ang_ready, sin_ready, wide_ready, tab_out, tab_ready) = sems(
             "set_up att_zero par_T par_ready std_ready rstd_ready xT_out h_hi h_ready row_out lb_arg "
             "lb_exp ang_ready sin_ready wide_ready tab_out tab_ready")
        (hg_sig, hg_arg, hg_ln, hg_G, hg_eG, hg_e16, hg_qs, hg_qin, hg_enG, hg_diff, hg_ed, hg_kq, hg_og,
         lev_out, lev_kq, lev_taken, hg_o, hg_sq, hg_sum, hg_ms, hg_std, hg_rs, hg_row, hg_yf, hg_hi, yc_ready) = sems(
             "hg_sig hg_arg hg_ln hg_G hg_eG hg_e16 hg_qs hg_qin hg_enG hg_diff hg_ed hg_kq hg_og "
             "lev_out lev_kq lev_taken hg_o hg_sq hg_sum hg_ms hg_std hg_rs hg_row hg_yf hg_hi yc_ready")
        (r_sw, r_rope, r_sc, r_att, r_g, r_o, r_sqd, r_ms, r_std, r_rs, r_row, r_yf, r_hi, ya_ready) = sems(
            "r_sw r_rope r_sc r_att r_g r_o r_sqd r_ms r_std r_rs r_row r_yf r_hi ya_ready")
        sv_T, sv_ready = sems("sv_T sv_ready")
        (s_sw, s_rope, s_kd, s_sc, s_arg, s_exp, s_prob, s_T, s_PT, s_o, s_hi, yb_ready) = sems(
            "s_sw s_rope s_kd s_sc s_arg s_exp s_prob s_T s_PT s_o s_hi yb_ready")
        g_in, g_sig, mix_sum, mix_hi, mix_ready = sems("g_in g_sig mix_sum mix_hi mix_ready")
        m_std, m_rs, m_norm, m_T, m_hi, m_ready = sems("m_std m_rs m_norm m_T m_hi m_ready")
        x_new, x_hi, x_sq, x_lo, x_acc, n_ms, n_std, n_rs, n_row, n_ready = sems(
            "x_new x_hi x_sq x_lo x_acc n_ms n_std n_rs n_row n_ready")
        a_sc, a_max, a_exp, a_prob, a_T, a_PT, a_o, a_hi, a_ready = sems(
            "a_sc a_max a_exp a_prob a_T a_PT a_o a_hi a_ready")
        f_tap = sems("f_tap0 f_tap1")
        f_z, f_conv, f_silu, f_prod, f_hi, f_ready = sems("f_z f_conv f_silu f_prod f_hi f_ready")
        o_new, o_sq, o_g, o_acc, o_T, o_tok, o_ms, o_std, o_fin = sems(
            "o_new o_sq o_g o_acc o_T o_tok o_ms o_std o_fin")

        block = ctx.enter_context(nc.Block())

        @block.sync
        def _(sp):
            def kp(w):
                return w.rearrange("(k p) c -> p k c", p=P)

            win, wout, wmq, wmkv = kp(w_in[0]), kp(w_out[0]), kp(w_mq[0]), kp(w_mkv[0])
            wmo, wup, wdn = kp(w_mo[0]), kp(w_up[0]), kp(w_down[0])
            wbr = [kp(w_branch[0, b]) for b in range(3)]

            def load(n, *pieces):
                if n.c >= 2:
                    sp.wait_ge(lo_ready, n.n(-1))
                for dst, src in pieces:
                    sp.dma_start(dst, src).then_inc(raw_in[n.s], 16)

            def load_pair(n, w, c0):
                v = raw[n.s][:, :].rearrange("p (k c) -> p k c", k=KD)
                load(n, *((v[:, k:k + 4, :], w[:, k:k + 4, bass.ds(c0, 256)]) for k in (0, 4)))

            def load_gate(n, b, j):
                v = raw[n.s][:, 0:12 * P].rearrange("p (k c) -> p k c", k=12)
                load(n, (v[:, 0:8, :], win[:, :, bass.ds(j * P + (C_GATE + b * D), P)]),
                     (v[:, 8:12, :], wbr[b][:, :, bass.ds(j * P, P)]))

            def load_mo(n, c0):
                v = raw[n.s][:, 0:4 * 256].rearrange("p (k c) -> p k c", k=4)
                load(n, *((v[:, k:k + 2, :], wmo[:, k:k + 2, bass.ds(c0, 256)]) for k in (0, 2)))

            def load_up(n, j):
                v = raw[n.s][:, :].rearrange("p (k h c) -> p h k c", k=KD, h=2)
                load(n, *((v[:, h], wup[:, :, bass.ds(j * P + h * FF, P)]) for h in (0, 1)))

            def load_down(n, j, half):
                v = raw[n.s][:, 0:KH * P].rearrange("p (k c) -> p k c", k=KH)
                load(n, *((v[:, a:b, :], wdn[:, KH * half + a:KH * half + b, bass.ds(j * P, P)])
                          for a, b in ((0, 6), (6, KH))))

            xsrc = x[0].rearrange("(t p) d -> p t d", p=P)
            sp.dma_start(xtok[:, 0, :], xsrc[:, 0, :]).then_inc(x_in[0], 16)
            sp.dma_start(ident[:, :], consts[:, K_ID:K_ID + P]).then_inc(ident_in, 16)
            def first_slot(half):
                v = raw[0][:, :].rearrange("p (k c) -> p k c", k=KD)
                k = slice(4 * half, 4 * half + 4)
                sp.dma_start(v[:, k, :], win[:, k, PAIRS[0]:PAIRS[0] + 256]).then_inc(first_in[half], 16)

            for t in range(1, NT):
                sp.dma_start(xtok[:, t, :], xsrc[:, t, :]).then_inc(x_in[t], 16)
            sp.dma_start(rows_gain[:, 0, :], norm_mix_g[0].rearrange("(k p) -> k p", p=P)).then_inc(par_in, 16)
            sp.dma_start(rows_gain[:, 1, :], norm_mem_g[0].rearrange("(k p) -> k p", p=P)).then_inc(par_in, 16)
            sp.dma_start(rows_gain[:, 2, :], mem_norm_g[0].rearrange("(k p) -> k p", p=P)).then_inc(par_in, 16)
            sp.dma_start(rows_gain[:, 3, :], norm_ffn_g[0].rearrange("(k p) -> k p", p=P)).then_inc(par_in, 16)
            sp.dma_start(rows_gain[:, 4, :], final_norm_g.rearrange("(k p) -> k p", p=P)).then_inc(par_in, 16)
            sp.dma_start(rows_hg[:, 0, :], hg_norm_g[0].rearrange("(k p) -> k p", p=P)).then_inc(par_in, 16)
            sp.dma_start(rows_hg[:, 1, :], hg_lb_logits[0].rearrange("(k p) -> k p", p=P)).then_inc(par_in, 16)
            sp.dma_start(rows_conv[:, 0:3, :],
                         conv_w[0].rearrange("j (k p) -> k j p", p=P)).then_inc(par_in, 16)
            sp.dma_start(rows_conv[:, 3, :], conv_b[0].rearrange("(k p) -> k p", p=P)).then_inc(par_in, 16)
            for half in range(2):
                first_slot(half)
            sp.dma_start(posi[:, :], positions[0].rearrange("(t p) -> p t", p=P),
                         allow_slow_non_contiguous=True).then_inc(const_in, 16)
            sp.dma_start(invf[:, :], consts[:, K_INV:K_INV + 32]).then_inc(const_in, 16)
            load_pair(Slot(1), win, PAIRS[1])
            sp.dma_start(masks[:, :, :],
                         consts[:, K_MASK:K_MASK + 4 * P].rearrange("p (i t) -> p i t", i=4)).then_inc(const_in, 16)
            sp.dma_start(decay[:, :, :],
                         consts[:, K_DECAY:K_DECAY + H * S].rearrange("p (h t) -> p h t", h=H)).then_inc(const_in, 16)
            sk4 = swa_sinks[0].rearrange("(v a r) -> a r v", v=2, a=2)
            for a in range(2):
                for r in range(2):
                    sp.dma_start(sinks[64 * a:64 * a + 64, r, :], sk4[a, r].partition_broadcast(64),
                                 allow_slow_non_contiguous=True).then_inc(const_in, 16)
            for c in range(2, N_G0):
                load_pair(Slot(c), win, PAIRS[c])
            for c in range(N_G0, N_LINE):
                load_gate(Slot(c), 2 if c < N_G1 else 0, (c - N_G0) % KD)
                if c == N_G0 + 8:
                    sp.wait_ge(ya_ready, 1)
                    sp.dma_start(memtok[:, :, :], mem[0].rearrange("(t p) d -> p t d", p=P)).then_inc(mem_in, 16)
            sp.wait_ge(slot_done, N_G1)
            sp.dma_start(xtok2[:, :, :], xsrc).then_inc(x2_in, 16)
            with sp.Fori(0, (N_G2 - N_LINE) // 2) as i:
                for k in range(2):
                    load_gate(Slot(N_LINE + k, i, 2), 0, i * 2 + (2 + k))
            with sp.Fori(0, KD // 2) as i:
                for k in range(2):
                    load_gate(Slot(N_G2 + k, i, 2), 1, i * 2 + k)
            for c in range(4):
                load_pair(Slot(N_OUT + c), wout, 256 * c)
            for c in range(2):
                load_pair(Slot(N_MK + 2 * c), wmkv, 256 * c)
                load_pair(Slot(N_MQ + 2 * c), wmq, 256 * c)
            for c in range(2):
                load_pair(Slot(N_MV + c), wmkv, BR + 256 * c)
            with sp.Fori(0, 2) as i:
                for k in range(2):
                    load_mo(Slot(N_MO + k, i, 2), i * 512 + 256 * k)
            with sp.Fori(0, KF // 2) as i:
                for k in range(2):
                    load_up(Slot(N_UP + k, i, 2), i * 2 + k)
            with sp.Fori(0, KD) as i:
                for k in range(2):
                    load_down(Slot(N_DN + k, i, 2), i, k)
            osrc = out[0].rearrange("(t p) d -> p t d", p=P)
            for t in range(NT):
                sp.wait_ge(o_fin, t + 1)
                sp.dma_start(osrc[:, t, :], otok[:, t, :]).then_inc(out_done, 16)
            sp.wait_ge(out_done, 16 * NT)

        @block.gpsimd
        def _(pool):
            for i in range(NT):
                pool.memset(att[i][:, :, :], 0.0).then_inc(att_zero, 1)
            for h in range(1, H):
                pool.wait_ge(hg_sq, h + 1)
                if h > 1:
                    pool.wait_ge(hg_sum, h - 1)
                pool.tensor_tensor(hgsq[:, 0, :], hgsq[:, 0, :], hgsq[:, h, :], ALU.add).then_inc(hg_sum, 1)
            pool.wait_ge(m_T, 4)
            for k in range(2 * KD):
                pool.wait_ge(x_sq, k + 1)
                if k % KD == 0:
                    if k:
                        pool.wait_ge(n_ms, 1)
                    pool.tensor_copy(ssqT[:, :], sqr[:, :]).then_inc(x_acc, 1)
                else:
                    pool.wait_ge(x_acc, k)
                    pool.tensor_tensor(ssqT[:, :], ssqT[:, :], sqr[:, :], ALU.add).then_inc(x_acc, 1)

        @block.tensor
        def _(pe):
            def product(out_ap, terms, done=None, start=True, stop=True, ready=None, first=1):
                for k, (lh, ll, rh, rl) in enumerate(terms):
                    if ready is not None:
                        pe.wait_ge(ready, first + k)
                    for m, (a, b) in enumerate(((lh, rh), (lh, rl), (ll, rh))):
                        last = pe.matmul(out_ap, a, b, start=start and k + m == 0,
                                         stop=stop and m == 2 and k == len(terms) - 1)
                if done is not None:
                    last.then_inc(done, 1)
                return last

            def enter(n, banks=True):
                pe.wait_ge(lo_ready, n.n(1))
                if banks and n.c >= 2:
                    pe.wait_ge(taken, n.n(-1))

            def weights(n, kt, cols):
                return (wH[n.s][:, 0:kt * cols].rearrange("p (k c) -> p k c", k=kt),
                        wL[n.s][:, 0:kt * cols].rearrange("p (k c) -> p k c", k=kt))

            def tile_product(n, c, kt, cols, k0, k1, xh, xl, done, xk0=0, width=S, ready=None, first=1):
                vh, vl = weights(n, kt, cols)
                b = 2 * n.s + c
                cc = P * c if cols > P else 0
                product(ps[:, b, 0:width],
                        [(vh[:, k, cc:cc + P], vl[:, k, cc:cc + P], xh[:, k - xk0, 0:width], xl[:, k - xk0, 0:width])
                         for k in range(k0, k1)], done, ready=ready, first=first)

            def pair_T(n, xh, xl, kt=KD, width=S, ready=None, first=1):
                enter(n)
                tile_product(n, 0, kt, 256, 0, kt, xh, xl, first_done, 0, width, ready, first)
                tile_product(n, 1, kt, 256, 0, kt, xh, xl, slot_done, 0, width)

            def pair_V(n, xh, xl, tiles=NT):
                enter(n)
                vh, vl = weights(n, KD, 256)
                for t in range(tiles):
                    b = 2 * n.s + (t // 2 if tiles == NT else t)
                    c0 = 256 * (t % 2) if tiles == NT else 0
                    f = slice(P * t, P * t + P)
                    done = {tiles // 2 - 1: first_done, tiles - 1: slot_done}.get(t)
                    product(ps[:, b, c0:c0 + 256],
                            [(xh[:, k, f], xl[:, k, f], vh[:, k, :], vl[:, k, :]) for k in range(KD)], done)

            def transposes(blocks, done):
                for out_ap, in_ap in blocks:
                    k = in_ap.shape[0]
                    last = pe.transpose(out_ap, in_ap, ident[0:k, 0:k])
                last.then_inc(done, 1)

            def rows_of(cols, bank, done):
                for t in range(NT):
                    last = pe.matmul(ps[:, bank, P * t:P * t + P], cols[:, t:t + 1].to_broadcast([P, P]), ident[:, :],
                                     start=True, stop=True)
                last.then_inc(done, 1)

            def column_sums(groups, bank, done):
                for c, tiles in enumerate(groups):
                    for m, a in enumerate(tiles):
                        last = pe.matmul(ps[:, bank, c:c + 1], a, ones[:, 0:1], start=m == 0,
                                         stop=m == len(tiles) - 1)
                last.then_inc(done, 1)

            def x_tile(t, k):
                return pe.transpose(ps[:, k, P * t:P * t + P], xtok[:, t, P * k:P * k + P], ident[:, :])

            pe.wait_ge(ident_in, 16)
            for t in range(NT):
                pe.wait_ge(x_in[t], 16)
                for k in range(KD - 1):
                    last = x_tile(t, k)
                    if t == NT - 1:
                        last.then_inc(xT_out, 1)
                if t == NT - 2:
                    pe.wait_ge(par_in, 9 * 16)
                    blocks = [(ps[:, KD - 1, R_CONV + 2 * KF * i:R_CONV + 2 * KF * (i + 1)], rows_conv[:, i, :])
                              for i in range(4)]
                    blocks += [(ps[:, KD - 1, R_GAIN + KD * i:R_GAIN + KD * (i + 1)], rows_gain[:, i, :])
                               for i in range(5)]
                    blocks += [(ps[:, KD - 1, R_HG + H * i:R_HG + H * (i + 1)], rows_hg[:, i, :]) for i in range(2)]
                    transposes(blocks, par_T)
            pe.wait_ge(par_ready, 1)
            for t in range(NT):
                last = x_tile(t, KD - 1)
            last.then_inc(xT_out, 1)

            def levels(li, ks, banks_free):
                k1, q0 = (L, L) if li == 3 else (P, 0)
                for i in range(NT):
                    pe.wait_ge(lev_taken, banks_free + i + 1)
                    for h in range(H):
                        w = P - q0
                        last = pe.matmul(ps[0:k1, 4 + i, w * h:w * h + w], ks[:, h, P * i:P * i + k1],
                                         hgQ[:, h, P * i + q0:P * i + P], start=True, stop=True)
                    last.then_inc(lev_out, 1)

            def values(v, done):
                for h in range(H):
                    for i in range(NT):
                        last = pe.matmul(ps[:, 4 + h, P * i:S], v[:, i, P * h:P * h + P], att[i][:, h, :],
                                         start=i == 0, stop=i == NT - 1)
                    last.then_inc(done, 1)

            def r_scores(h, i, bank, c0):
                r = slice(64 * (h % 2), 64 * (h % 2) + 64)
                return pe.matmul(ps[:, bank, c0:c0 + S - P * i], rqk[r, 2 + h // 2, P * i:P * i + P],
                                 rqk[r, h // 2, P * i:S], start=True, stop=True)

            def s_scores(hf):
                for cp in range(2):
                    for r in range(2):
                        rows = slice(64 * r, 64 * r + 64)
                        for cm in range(2):
                            c = 4 * hf + 2 * cp + cm
                            for v in range(2):
                                q = sqc[rows, v, c].rearrange("p a t -> p (a t)")
                                o = ps[:, 4 + 2 * cp + r, 256 * cm + 128 * v:256 * cm + 128 * v + 128]
                                if cm:
                                    last = pe.matmul(o, q, kd[rows, v, L * (c - 1):L * (c + 1)], start=True, stop=True)
                                else:
                                    odd = max(c - 1, 0)
                                    pe.matmul(o[:, 0:L], q, kd[rows, v, L * c:L * c + L], start=True, stop=True)
                                    last = pe.matmul(o[:, L:2 * L], q, kd[rows, v, L * odd:L * odd + L],
                                                     start=True, stop=True)
                last.then_inc(s_sc, 1)

            def s_values(hf):
                for u in range(16):
                    cp, r, cm, v = u // 8, u // 4 % 2, u // 2 % 2, u % 2
                    c = 4 * hf + 2 * cp + cm
                    band = sv[:, c // 2, :] if cm else vb[:, c // 2, :]
                    k = L if c == 0 else P
                    o = ps[64 * r:64 * r + 64, 4 + v, :].rearrange("p (a t) -> p a t", a=2)
                    last = pe.matmul(o[:, :, L * (c % 4):L * (c % 4) + L], band[0:k, 64 * v:64 * v + 64],
                                     sPT[0:k, u, :].rearrange("p (a t) -> p a t", a=2), start=True, stop=True)
                last.then_inc(s_o, 1)

            def job(n):
                if n == 0:
                    pe.wait_ge(rstd_ready, 1)
                    rows_of(rstd, 4, row_out)
                elif n == 1:
                    pe.wait_ge(wide_ready, 1)
                    for i in range(2):
                        transposes([(ps[:, 5 + i, P * t:P * t + P],
                                            wide[:, i, t].rearrange("p q f -> p (q f)")) for t in range(NT)], tab_out)
                elif n == 5:
                    pe.wait_ge(hg_kq, 1)
                    pe.wait_ge(tab_ready, 2)
                    for i in range(NT):
                        for h in range(H):
                            f = slice(P * i, P * i + P)
                            last = pe.matmul(ps[:, 4 + i, P * h:P * h + P], hgK[:, h, f], hgQ[:, h, f],
                                             start=True, stop=True)
                        last.then_inc(lev_out, 1)
                elif n == 6:
                    pe.wait_ge(hg_kq, 2)
                    levels(1, hgF, 0)
                elif n == 7:
                    pe.wait_ge(lev_kq, 1)
                    levels(2, hgF, 4)
                elif n == 8:
                    pe.wait_ge(lev_kq, 2)
                    levels(3, hgF, 8)
                elif n == 9:
                    pe.wait_ge(lev_kq, 3)
                    for m, i in enumerate((0, 2)):
                        pe.wait_ge(lev_taken, 13 + m)
                        for h in range(H):
                            last = pe.matmul(ps[:, 4 + m, P * h:P * h + P], hgF[:, h, P * i:P * i + P],
                                             hgQ[:, h, P * i + P:P * i + 2 * P], start=True, stop=True)
                        last.then_inc(lev_out, 1)
                elif n == 10:
                    pe.wait_ge(lev_kq, 4)
                    pe.wait_ge(lev_taken, 18)
                    for m in range(4):
                        i = m // 2
                        for h in (2 * (m % 2), 2 * (m % 2) + 1):
                            last = pe.matmul(ps[:, 4 + m, 256 * (h % 2):256 * (h % 2) + 256],
                                             hgF[:, h, P * i:P * i + P], hgQ[:, h, 2 * P:S], start=True, stop=True)
                        last.then_inc(lev_out, 1)
                elif n == 11:
                    pe.wait_ge(lev_taken, 22)
                    values(hgV, hg_o)
                elif n == 12:
                    pe.wait_ge(hg_sum, H - 1)
                    column_sums([[hgsq[:, 0, P * t:P * t + P]] for t in range(NT)], 4, hg_ms)
                elif n == 13:
                    pe.wait_ge(hg_rs, 1)
                    rows_of(statr, 4, hg_row)
                elif n == 14:
                    pe.wait_ge(hg_yf, 1)
                    pe.wait_ge(r_rope, 1)
                    for h in range(H):
                        r_scores(h, 0, 4 + h, 0).then_inc(r_sc, 1)
                elif n == 15:
                    for h in range(H):
                        pe.wait_ge(r_att, h + 1)
                        r_scores(h, 1, 4 + h, 0).then_inc(r_sc, 1)
                elif n == 16:
                    pe.wait_ge(r_att, 8)
                    for i, b0 in ((2, 4), (3, 6)):
                        for r in range(2):
                            r_scores(r, i, b0 + r, 0)
                            r_scores(r + 2, i, b0 + r, 256).then_inc(r_sc, 1)
                elif n == 17:
                    pe.wait_ge(r_att, 12)
                    values(rV, r_o)
                elif n == 18:
                    pe.wait_ge(r_sqd, H)
                    column_sums([[rsq[:, h, P * t:P * t + P]] for h in range(H) for t in range(NT)], 4, r_ms)
                    pe.wait_ge(taken, 17)
                    transposes([(ps[:, 5, P * t:P * t + P], svT[:, P * t:P * t + P]) for t in range(NT)], sv_T)
                elif n == 19:
                    pe.wait_ge(r_rs, 1)
                    pe.wait_ge(sv_ready, 1)
                    for h in range(H):
                        rows_of(statr[:, 4 * h:4 * h + 4], 4 + h, r_row)
                elif n == 20:
                    pe.wait_ge(r_yf, 1)
                    pe.wait_ge(s_rope, 3)
                    pe.wait_ge(s_kd, 1)
                    s_scores(0)
                elif n == 21:
                    pe.wait_ge(s_arg, 1)
                    s_scores(1)
                elif n in (22, 24):
                    hf = (n - 22) // 2
                    pe.wait_ge(s_arg, 2)
                    pe.wait_ge(s_prob, hf + 1)
                    if hf:
                        pe.wait_ge(yb_ready, 1)
                    for b in range(4):
                        transposes([(ps[:, 4 + b, P * (u % 4):P * (u % 4) + P], sP[hf][:, u, :])
                                           for u in range(4 * b, 4 * b + 4)], s_T)
                elif n in (23, 25):
                    hf = (n - 23) // 2
                    pe.wait_ge(s_PT, 4 * hf + 4)
                    s_values(hf)
                elif n == 26:
                    pe.wait_ge(m_norm, 1)
                    pe.wait_ge(yb_ready, 2)
                    for b in range(4):
                        transposes([(ps[:, 4 + b, 256 * e + P * t:256 * e + P * t + P],
                                            memtok[:, t, P * (2 * b + e):P * (2 * b + e) + P])
                                           for e in range(2) for t in range(MT)], m_T)

            for c in range(N_G0):
                n = Slot(c)
                if c in (4, 5, 10, 11):
                    pair_V(n, hH, hL)
                elif c < N_G0 - 1:
                    if c:
                        pair_T(n, hH, hL)
                    else:
                        pe.wait_ge(half_ready, 1)
                        vh, vl = weights(n, KD, 256)
                        for half in range(2):
                            ks = range(4 * half, 4 * half + 4)
                            if half:
                                pe.wait_ge(lo_ready, 1)
                            product(ps[:, 0, :], [(vh[:, k, 0:P], vl[:, k, 0:P], hH[:, k, :], hL[:, k, :]) for k in ks],
                                    first_done if half else None, half == 0, half == 1, h_ready, ks[0] + 1)
                        tile_product(n, 1, KD, 256, 0, KD, hH, hL, slot_done)
                else:
                    pair_T(n, hH, hL)
                job(c)

            def gate_and_branch(n, yh, yl, between=None):
                enter(n)
                tile_product(n, 0, 12, P, 0, KD, hH, hL, first_done)
                if between is not None:
                    between()
                tile_product(n, 1, 12, P, KD, 12, yh, yl, slot_done, KD)

            for c in range(N_G0, N_LINE):
                if c == N_G0:
                    pe.wait_ge(yc_ready, 1)
                if c == N_G1:
                    pe.wait_ge(ya_ready, 1)
                yh, yl = (ycH, ycL) if c < N_G1 else (yaH, yaL)
                gate_and_branch(Slot(c), yh, yl, (lambda: job(22)) if c == 23 else None)
                if c != 22:
                    job(c)
            with pe.Fori(0, (N_G2 - N_LINE) // 2) as i:
                for k in range(2):
                    gate_and_branch(Slot(N_LINE + k, i, 2), yaH, yaL)
            with pe.Fori(0, KD // 2) as i:
                for k in range(2):
                    gate_and_branch(Slot(N_G2 + k, i, 2), ybH, ybL)
            for c in range(4):
                n = Slot(N_OUT + c)
                enter(n)
                vh, vl = weights(n, KD, 256)

                def projected(e):
                    product(ps[:, 2 * n.s + e, :],
                            [(vh[:, k, P * e:P * e + P], vl[:, k, P * e:P * e + P], mixH[:, k, :], mixL[:, k, :])
                             for k in range(KD)], stop=False, ready=None if c or e else mix_ready)

                def residual(e):
                    d0 = P * (2 * c + e)
                    for t in range(NT):
                        last = pe.matmul(ps[:, 2 * n.s + e, P * t:P * t + P], xtok2[:, t, d0:d0 + P], ident[:, :],
                                         start=False, stop=t == NT - 1)
                    last.then_inc((first_done, slot_done)[e], 1)

                if c == 0:
                    pe.wait_ge(x2_in, 16)
                for e in range(2):
                    projected(e)
                    residual(e)
            def a_scores(h):
                if h:
                    pe.wait_ge(a_exp, h)
                for t in range(NT):
                    last = pe.matmul(ps[:, 4 + t // 2, 256 * (t % 2):256 * (t % 2) + 256], mq[:, h, P * t:P * t + P],
                                     mkT[:, h, :], start=True, stop=True)
                last.then_inc(a_sc, 1)

            def a_transposes(h):
                pe.wait_ge(a_prob, h + 1)
                if h:
                    pe.wait_ge(a_PT, 2 * h)
                for m in range(MT):
                    transposes([(ps[:, 6 + m, P * t:P * t + P], mP[h % 2][:, t, P * m:P * m + P])
                                       for t in range(NT)], a_T)

            def a_values(h):
                pe.wait_ge(a_PT, 2 * h + 2)
                for m in range(MT):
                    last = pe.matmul(ps[:, h ^ 2, :], mV[:, m, P * h:P * h + P], mPT[h % 2][:, m, :], start=m == 0,
                                     stop=m == MT - 1)
                last.then_inc(a_o, 1)

            pe.wait_ge(m_ready, KD // 2)
            pair_T(Slot(N_MK), memH, memL, width=M)
            pe.wait_ge(x_acc, KD)
            column_sums([[ssqT[:, P * t:P * t + P]] for t in range(NT)], 4, n_ms)
            pair_T(Slot(N_MQ), hH, hL, ready=x_lo)
            pe.wait_ge(n_rs, 1)
            rows_of(rstd, 5, n_row)
            pair_T(Slot(N_MK + 2), memH, memL, width=M)
            pe.wait_ge(taken, N_MQ + 1)
            pe.wait_ge(n_ready, 1)
            a_scores(0)
            n = Slot(N_MQ + 2)
            enter(n)
            tile_product(n, 0, KD, 256, 0, KD, hH, hL, first_done)
            a_scores(1)
            tile_product(n, 1, KD, 256, 0, KD, hH, hL, slot_done)
            a_transposes(0)
            pair_V(Slot(N_MV), memH, memL, MT)
            pe.wait_ge(taken, N_MV)
            a_scores(2)
            a_transposes(1)
            pair_V(Slot(N_MV + 1), memH, memL, MT)
            a_scores(3)
            pe.wait_ge(taken, N_MO)
            a_values(0)
            a_transposes(2)
            a_values(1)
            a_transposes(3)
            a_values(2)
            a_values(3)
            for c in range(4):
                n = Slot(N_MO + c)
                if c == 0:
                    enter(n)
                    pe.wait_ge(a_ready, 2)
                    vh, vl = weights(n, KB, 256)
                    for heads in (range(H - 1), (H - 1,)):
                        for e, done in ((0, first_done), (1, slot_done)):
                            e = slice(P * e, P * e + P)
                            last = H - 1 in heads
                            product(ps[:, 2 * n.s + e.start // P, :],
                                    [(vh[:, k, e], vl[:, k, e], moH[:, k, :], moL[:, k, :]) for k in heads],
                                    done if last else None, start=not last, stop=last, ready=a_ready,
                                    first=heads[0] + 1)
                else:
                    if c == 1:
                        pe.wait_ge(a_ready, H)
                    pair_T(n, moH, moL, KB)

            def up(n, ready=None, first=1, then=None):
                enter(n)
                tile_product(n, 0, KD, 256, 0, KD, hH, hL, first_done, ready=ready, first=first)
                if then is not None:
                    then()
                tile_product(n, 1, KD, 256, 0, KD, hH, hL, slot_done)

            def sums():
                pe.wait_ge(x_acc, 2 * KD)
                column_sums([[ssqT[:, P * t:P * t + P]] for t in range(NT)], 4, n_ms)

            up(Slot(N_UP), x_lo, KD + 1, sums)
            pe.wait_ge(n_rs, 2)
            rows_of(rstd, 5, n_row)
            up(Slot(N_UP + 1))
            with pe.Fori(0, KF // 2 - 1) as i:
                for k in range(2):
                    up(Slot(N_UP + 2 + k, i, 2))

            def down_half(n, q, half, ready=None):
                enter(n, banks=False)
                vh, vl = weights(n, KH, P)
                product(ps[:, 4 + q, :],
                        [(vh[:, k, :], vl[:, k, :], actH[:, KH * half + k, :], actL[:, KH * half + k, :])
                         for k in range(KH)], slot_done, start=half == 0, stop=half == 1, ready=ready, first=KH + 1)

            def back(m, q):
                pe.wait_ge(o_g, m.n(1))
                if m.c >= 2:
                    pe.wait_ge(o_tok, m.n(-1))
                transposes([(ps[:, 6 + q, P * t:P * t + P], xg[:, P * t:P * t + P]) for t in range(NT)], o_T)

            def down_tile(m, q):
                n = Slot(N_DN + 2 * m.c, m.i, 2 * m.per)
                if m.c >= 2:
                    pe.wait_ge(o_new, m.n(-1))
                down_half(n, q, 0)
                if m.c >= 1:
                    back(m + -1, 1 - q)
                down_half(n + 1, q, 1, None if m.c else f_ready)

            pe.wait_ge(f_ready, KH)
            pe.wait_ge(n_ready, 2)
            down_tile(Slot(0), 0)
            down_tile(Slot(1), 1)
            with pe.Fori(0, KD // 2 - 1) as i:
                for q in range(2):
                    down_tile(Slot(2 + q, i, 2), q)
            pe.wait_ge(o_acc, KD - 1)
            for t in range(NT):
                pe.matmul(ps[:, t, 0:1], ssqF[:, P * t:P * t + P], ones[:, 0:1], start=True, stop=False)
            back(Slot(KD - 1), 1)
            pe.wait_ge(o_sq, KD)
            for t in range(NT):
                last = pe.matmul(ps[:, t, 0:1], fsq[:, P * t:P * t + P], ones[:, 0:1], start=False, stop=True)
            last.then_inc(o_ms, 1)

        @block.scalar
        def _(act):
            q = Order(act, act_step)

            def do(out_ap, in_ap, fn, sem=None, **kw):
                q.sig(act.activation(out_ap, in_ap, fn, **kw), sem)

            def hi(n, width=2048):
                act.wait_ge(raw_in[n.s], n.loads())
                if n.c >= 2:
                    act.wait_ge(slot_done, n.n(-1))
                do(wH[n.s][:, 0:width], raw[n.s][:, 0:width], ACT.Copy, hi_ready)

            def square_sum(t):
                act.wait_ge(x_in[t], 16)
                if t:
                    q.settle()
                do(junk[:, :], xtok[:, t, :], ACT.Square, accum_out=ssq[:, t:t + 1])

            act.wait_ge(set_up, 1)
            for t in range(NT - 1):
                square_sum(t)

            def first_hi(half):
                act.wait_ge(first_in[half], 16)
                f = slice(1024 * half, 1024 * half + 1024)
                do(wH[0][:, f], raw[0][:, f], ACT.Copy, (first_half, hi_ready)[half])

            first_hi(0)
            act.wait_ge(par_ready, 1)
            for k in range(KD):
                if k == 2:
                    first_hi(1)
                act.wait_ge(xT_out, k + 1)
                do(hH[:, k, :], ps[:, k, :], ACT.Copy, h_hi, scale=par[:, G_MIX + k:G_MIX + k + 1])
            hi(Slot(1))
            square_sum(NT - 1)
            q.settle()
            do(rstd[:, NT:2 * NT], ssq[:, 0:NT], ACT.Sqrt, std_ready, scale=1.0 / D, bias=eps[:, 0:1])
            act.wait_ge(lb_arg, 1)
            do(lbt[:, 1, :], lbt[:, 0, :], ACT.Exp, lb_exp)
            act.wait_ge(ang_ready, 1)
            do(trig[:, 0], ang[:, :, :], ACT.Sin, sin_ready, scale=0.5)
            do(trig[:, 1], ang[:, :, :], ACT.Sin, sin_ready)

            def swaps(dst, src, done):
                for b in range(4):
                    o = 32 * (b ^ 1)
                    do(dst[32 * b:32 * b + 32], src[o:o + 32], ACT.Copy, done)

            def job(n):
                if n == 2:
                    act.wait_ge(taken, 2)
                    do(hgF[:, :, :], hgF[:, :, :], ACT.Sigmoid, hg_sig)
                elif n == 3:
                    act.wait_ge(hg_arg, 2)
                    do(hgF[:, :, :], hgF[:, :, :], ACT.Ln, hg_ln)
                    do(hgl[:, :, :], hgl[:, :, :], ACT.Ln, hg_ln)
                    act.wait_ge(hg_G, H)
                    do(hgK[:, :, :], hgG[:, :, :], ACT.Exp, hg_eG)
                    do(e16[:, :, :], hgG[:, :, :].rearrange("p h (n t) -> p h n t", t=HG_T)[:, :, :, HG_T - 1],
                       ACT.Exp, hg_e16)
                    act.wait_ge(hg_diff, 1)
                    do(hgF[:, :, :], hgF[:, :, :], ACT.Exp, hg_ed)
                elif n == 4:
                    act.wait_ge(taken, 4)
                    do(hgQ[:, :, :], hgQ[:, :, :], ACT.Silu, hg_qs)
                    act.wait_ge(hg_qin, 1)
                    do(hgK[:, :, :], hgG[:, :, :], ACT.Exp, hg_enG, scale=-1.0)
                elif n == 8:
                    act.wait_ge(taken, 8)
                    do(hgO[:, :, :], hgO[:, :, :], ACT.Silu, hg_og)
                elif n == 10:
                    act.wait_ge(taken, 10)
                    swaps(rsw, rqk, r_sw)
                elif n == 12:
                    act.wait_ge(lev_taken, 22)
                    for h in range(H):
                        act.wait_ge(hg_o, h + 1)
                        do(hgY[:, h, :], ps[:, 4 + h, :], ACT.Copy)
                        do(hgsq[:, h, :], ps[:, 4 + h, :], ACT.Square, hg_sq)
                elif n == 13:
                    act.wait_ge(hg_ms, 1)
                    do(stat[:, 0:NT], ps[:, 4, 0:NT], ACT.Sqrt, hg_std, scale=1.0 / (H * P), bias=eps[:, 0:1])
                elif n == 14:
                    act.wait_ge(hg_yf, 1)
                    do(ycH[:, :, :], hgY[:, :, :], ACT.Copy, hg_hi)
                elif n == 15:
                    act.wait_ge(taken, 14)
                    do(rG[:, :, :], rG[:, :, :], ACT.Silu, r_g)
                elif n == 17:
                    act.wait_ge(taken, 16)
                    swaps(ssw, sq, s_sw)
                    act.wait_ge(taken, 17)
                    act.wait_ge(r_att, 12)
                    swaps(ssk, sk, s_sw)
                elif n == 18:
                    for h in range(H):
                        act.wait_ge(r_o, h + 1)
                        do(rY[:, h, :], ps[:, 4 + h, :], ACT.Copy)
                        do(rsq[:, h, :], ps[:, 4 + h, :], ACT.Square, r_sqd)
                elif n == 19:
                    act.wait_ge(r_ms, 1)
                    do(stat[:, :], ps[:, 4, 0:16], ACT.Sqrt, r_std, scale=1.0 / P, bias=eps[:, 0:1])
                    act.wait_ge(s_rope, 1)
                    for v in range(2):
                        for r in range(2):
                            do(kd[64 * r:64 * r + 64, v, :], sk[64 * v:64 * v + 64, :], ACT.Copy)
                    act.wait_ge(sv_ready, 1)
                    do(vb[0:64, :, :], sv[0:64, :, :], ACT.Copy)
                    do(vb[64:128, 1:NT, :], sv[64:128, 0:NT - 1, :], ACT.Copy, s_kd)
                elif n == 20:
                    act.wait_ge(r_yf, 1)
                    do(yaH[:, :, :], rY[:, :, :], ACT.Copy, r_hi)
                elif n in (21, 22):
                    hf = n - 21
                    act.wait_ge(s_arg, hf + 1)
                    do(sP[hf][:, :, :], sP[hf][:, :, :], ACT.Exp)
                    do(snk[:, hf, :], snk[:, hf, :], ACT.Exp, s_exp)
                if n in (23, 25):
                    hf = (n - 23) // 2
                    for b in range(4):
                        act.wait_ge(s_T, 4 * hf + b + 1)
                        do(sPT[:, 4 * b:4 * b + 4, :], ps[:, 4 + b, :].rearrange("p (u t) -> p u t", u=4), ACT.Copy,
                           s_PT)
                if n in (24, 26):
                    hf = (n - 24) // 2
                    act.wait_ge(s_o, hf + 1)
                    do(ybH[:, :, 256 * hf:256 * hf + 256], ps[:, 4:6, :].rearrange("p v (a t) -> p (v a) t", a=2),
                       ACT.Copy, s_hi)
                if n == 25:
                    act.wait_ge(mem_in, 16)
                    for t in range(MT):
                        if t:
                            q.settle()
                        do(mjunk[:, :], memtok[:, t, :], ACT.Square, accum_out=memst[:, t:t + 1])
                    q.settle()
                    do(memst[:, 2:4], memst[:, 0:2], ACT.Sqrt, m_std, scale=1.0 / D, bias=eps[:, 0:1])
                    act.wait_ge(m_rs, 1)
                    for t in range(MT):
                        do(memtok[:, t, :], memtok[:, t, :], ACT.Copy, m_norm if t else None,
                           scale=memst[:, 4 + t:5 + t])

            def gate_sigmoid(n):
                act.wait_ge(g_in, n.n(1 - N_G0))
                do(gate[n.s][:, :], gate[n.s][:, :], ACT.Sigmoid, g_sig)

            for c in range(N_LINE):
                if c:
                    hi(Slot(c + 1), 2048 if c + 1 < N_G0 else 12 * P)
                job(c)
                if c >= N_G0:
                    gate_sigmoid(Slot(c))
            for b in range(4):
                act.wait_ge(m_T, b + 1)
                for e in range(2):
                    do(memH[:, 2 * b + e, :], ps[:, 4 + b, 256 * e:256 * e + 256], ACT.Copy, m_hi,
                       scale=par[:, G_MEMN + 2 * b + e:G_MEMN + 2 * b + e + 1])
            turns = (N_G2 - N_LINE) // 2
            with act.Fori(0, turns) as i:
                q.enter(i, [(hi_ready, 2), (g_sig, 2)])
                for k in range(2):
                    n = Slot(N_LINE + k, i, 2)
                    hi(n + 1, 12 * P)
                    gate_sigmoid(n)
                q.leave(turns)

            def mix_upper(n):
                j = n.n(-N_G2)
                act.wait_ge(mix_sum, n.n(1 - N_G2))
                do(mixH[:, bass.ds(j, 1), :], mix[:, bass.ds(j, 1), :], ACT.Copy, mix_hi)

            turns = KD // 2
            with act.Fori(0, turns) as i:
                q.enter(i, [(hi_ready, 2), (g_sig, 2), (mix_hi, 2)])
                for k in range(2):
                    n = Slot(N_G2 + k, i, 2)
                    hi(n + 1, 2048)
                    gate_sigmoid(n)
                    mix_upper(n)
                q.leave(turns)

            def new_x(n, c, e, gain, between=None):
                if c == 0:
                    act.wait_ge(x_new, n)
                else:
                    act.wait_ge(taken, n)
                j = e.n(0 if gain == G_MEM else -KD)
                t = xT[:, j, :]
                do(hH[:, j, :], t, ACT.Copy, x_hi, scale=par[:, gain + j:gain + j + 1])
                if between is not None:
                    between()
                if e.c:
                    act.wait_ge(x_acc, e.n())
                do(sqr[:, :], t, ACT.Square, x_sq)

            for c in range(4):
                n = Slot(N_OUT + c)
                hi(n + 1)
                for e in range(2):
                    new_x(n.n(1 - N_OUT) if e == 0 else n.n(1), e, Slot(2 * c + e), G_MEM)
            hi(Slot(N_MQ))
            act.wait_ge(n_ms, 1)
            do(rstd[:, NT:2 * NT], ps[:, 4, 0:NT], ACT.Sqrt, n_std, scale=1.0 / D, bias=eps[:, 0:1])
            hi(Slot(N_MK + 2))
            hi(Slot(N_MQ + 2))
            hi(Slot(N_MV))
            scale = float(P) ** -0.5

            def a_exps(h):
                act.wait_ge(a_max, h + 1)
                if h >= 2:
                    act.wait_ge(a_T, 2 * h - 2)
                for t in range(NT):
                    do(mP[h % 2][:, t, :], ps[:, 4 + t // 2, 256 * (t % 2):256 * (t % 2) + 256], ACT.Exp,
                       a_exp if t == NT - 1 else None, scale=scale, bias=mstat[:, 1, h, t:t + 1],
                       accum_out=mstat[:, 2, h, t:t + 1])

            def a_transposed(h):
                for m in range(MT):
                    act.wait_ge(a_T, 2 * h + m + 1)
                    if h >= 2:
                        act.wait_ge(a_o, h - 1)
                    do(mPT[h % 2][:, m, :], ps[:, 6 + m, :], ACT.Copy, a_PT)

            def a_upper(h):
                act.wait_ge(a_o, h + 1)
                do(moH[:, h, :], ps[:, h ^ 2, :], ACT.Copy, a_hi)

            a_exps(0)
            a_exps(1)
            hi(Slot(N_MV + 1))
            a_transposed(0)
            hi(Slot(N_MO), 4 * 256)
            a_exps(2)
            a_transposed(1)
            hi(Slot(N_MO + 1), 4 * 256)
            a_exps(3)
            a_upper(0)
            a_transposed(2)
            a_upper(1)
            a_transposed(3)
            a_upper(2)
            a_upper(3)
            for c in range(4):
                n = Slot(N_MO + c)
                new_x(n.n(1 - N_MO + 4), 0, Slot(KD + 2 * c), G_FFN)
                if c == 2:
                    hi(n + 2)
                new_x(n.n(1), 1, Slot(KD + 2 * c + 1), G_FFN,
                      None if c == 2 else lambda: hi(n + 2, 4 * 256 if c < 2 else 2048))

            def ffn(n):
                def tap(e):
                    w = [par[:, bass.ds(n.n(R_CONV + 2 * KF * j + KF * e - N_UP), 1)] for j in (2, 3)]
                    do((ca, cu)[e][:, :], (za, zu)[e][:, 2:S + 2], ACT.Identity, f_tap[e], scale=w[0], bias=w[1])

                act.wait_ge(f_z, n.n(1 - N_UP))
                tap(0)
                act.wait_ge(f_conv, n.n(1 - N_UP))
                do(ca[:, :], ca[:, :], ACT.Silu, f_silu)
                act.wait_ge(taken, n.n(1))
                tap(1)
                hi(n + 2)
                act.wait_ge(f_prod, n.n(1 - N_UP))
                do(actH[:, bass.ds(n.n(-N_UP), 1), :], prod[:, :], ACT.Copy, f_hi)

            act.wait_ge(n_ms, 2)
            do(rstd[:, NT:2 * NT], ps[:, 4, 0:NT], ACT.Sqrt, n_std, scale=1.0 / D, bias=eps[:, 0:1])
            ffn(Slot(N_UP))
            ffn(Slot(N_UP + 1))
            turns = KF // 2 - 1
            with act.Fori(0, turns) as i:
                q.enter(i, [(hi_ready, 2), (f_tap[0], 2), (f_tap[1], 2), (f_silu, 2), (f_hi, 2)])
                for k in range(2):
                    ffn(Slot(N_UP + 2 + k, i, 2))
                q.leave(turns)

            def result(m, qq):
                act.wait_ge(o_new, m.n(1))
                if m.c:
                    act.wait_ge(o_acc, m.n())
                do(fsq[:, :], xT[:, bass.ds(m.n(), 1), :], ACT.Square, o_sq)

            def to_frames(m, qq):
                act.wait_ge(o_T, m.n(1))
                do(otok[:, :, bass.ds(m.n() * P, P)], ps[:, 6 + qq, :].rearrange("p (t d) -> p t d", t=NT), ACT.Copy,
                   o_tok)

            def down_tile(m, qq):
                n = Slot(N_DN + 2 * m.c, m.i, 2 * m.per)
                if m.c < KD - 1:
                    hi(n + 2, KH * P)
                if m.c:
                    to_frames(m + -1, 1 - qq)
                if m.c < KD - 1:
                    hi(n + 3, KH * P)
                result(m, qq)

            act.wait_ge(f_ready, KF)
            down_tile(Slot(0), 0)
            down_tile(Slot(1), 1)
            turns = KD // 2 - 2
            with act.Fori(0, turns) as i:
                q.enter(i, [(hi_ready, 4), (o_tok, 2), (o_sq, 2)])
                for k in range(2):
                    down_tile(Slot(2 + k, i, 2), k)
                q.leave(turns)
            down_tile(Slot(KD - 2), 0)
            do(eps[:, 1:2], eps[:, 0:1], ACT.Sqrt)
            down_tile(Slot(KD - 1), 1)
            to_frames(Slot(KD - 1), 1)
            act.wait_ge(o_ms, 1)
            do(rstd[:, NT:2 * NT], ps[:, 0:NT, 0], ACT.Sqrt, o_std, scale=1.0 / D, bias=eps[:, 0:1])

        @block.vector
        def _(dve):
            q = Order(dve, dve_step)

            def tt(out_ap, a, b, op, sem=None):
                q.sig(dve.tensor_tensor(out_ap, a, b, op), sem)

            def ts(out_ap, a, s1, s2, op0, op1=None, sem=None):
                q.sig(dve.tensor_scalar(out_ap, a, s1, s2, op0, op1) if op1 is not None
                      else dve.tensor_scalar(out_ap, a, s1, None, op0), sem)

            def stt(out_ap, a, s, b, op0, op1, sem=None):
                q.sig(dve.scalar_tensor_tensor(out_ap, a, s, b, op0, op1), sem)

            def copy(out_ap, a, sem=None):
                q.sig(dve.tensor_copy(out_ap, a), sem)

            def lo(n, width=2048):
                dve.wait_ge(hi_ready, n.n(1))
                tt(wL[n.s][:, 0:width], raw[n.s][:, 0:width], wH[n.s][:, 0:width].bitcast(F32), ALU.subtract, lo_ready)

            q.sig(dve.memset(ones[:, :], 1.0))
            q.sig(dve.memset(restart[:, :], 1.0))
            q.settle()
            q.sig(dve.memset(restart[:, :].rearrange("p (n t) -> p n t", t=HG_T)[:, :, 0:1], 0.0))
            q.sig(dve.memset(eps[:, :], EPS), set_up)
            dve.wait_ge(par_T, 1)
            copy(par[:, :], ps[:, KD - 1, 0:R_ALL], par_ready)
            q.settle()
            logits = par[:, R_HG + H:R_HG + 2 * H]
            tt(lbt[:, 0, :], logits, logits, ALU.subtract, lb_arg)

            def first_lo(half):
                dve.wait_ge((first_half, hi_ready)[half], 1)
                f = slice(1024 * half, 1024 * half + 1024)
                tt(wL[0][:, f], raw[0][:, f], wH[0][:, f].bitcast(F32), ALU.subtract, (half_ready, lo_ready)[half])

            first_lo(0)
            for k in range(KD):
                if k == 2:
                    first_lo(1)
                dve.wait_ge(h_hi, k + 1)
                stt(hL[:, k, :], ps[:, k, :], par[:, G_MIX + k:G_MIX + k + 1], hH[:, k, :].bitcast(F32),
                    ALU.mult, ALU.subtract, h_ready)
            lo(Slot(1))
            dve.wait_ge(std_ready, 1)
            q.sig(dve.reciprocal(rstd[:, 0:NT], rstd[:, NT:2 * NT]), rstd_ready)
            dve.wait_ge(const_in, 8 * 16)
            copy(posf[:, :], posi[:, :])
            q.settle()
            for t in range(NT):
                ts(ang[:, t, :], invf[:, :], posf[:, t:t + 1], None, ALU.mult)
            parts = split_two_pi()

            def whole_turns(dst, f):
                q.settle()
                ts(dst[:, :, :], ang[:, :, :], 1.0 / (2 * np.pi * f), MAGIC, ALU.mult, ALU.add)
                q.settle()
                ts(dst[:, :, :], dst[:, :, :], MAGIC, None, ALU.subtract)

            def take_off(dst, f, some):
                for part in some:
                    q.settle()
                    stt(ang[:, :, :], dst[:, :, :], -part * f, ang[:, :, :], ALU.mult, ALU.add)

            steps = list(zip(whole, (2.0 ** 22, 2.0 ** 11, 1.0)))
            for dst, f in steps:
                whole_turns(dst, f)
                take_off(dst, f, parts[:2])
            for dst, f in steps:
                take_off(dst, f, parts[2:])
            whole_turns(whole[0], 1.0)
            take_off(whole[0], 1.0, parts)
            q.settle()
            ts(ang[:, :, :], ang[:, :, :], float(np.float32(3.1415925)), -float(np.float32(3.1415925)), ALU.min,
               ALU.max, ang_ready)
            dve.wait_ge(lb_exp, 1)
            q.sig(dve.reciprocal(lbt[:, 0, :], lbt[:, 1, :]))
            q.settle()
            tt(lbt[:, 0, :], lbt[:, 0, :], lbt[:, 1, :], ALU.mult)
            q.settle()
            tt(lb[:, 0, :], lbt[:, 0, :], lbt[:, 0, :], ALU.subtract)
            q.settle()
            ts(lb[:, 1, :], lb[:, 0, :], -1.0, 1.0, ALU.mult, ALU.add)
            for cp in range(2):
                for cm in range(2):
                    copy(sink16[:, cp, :, cm, :], sinks[:, :, :])

            def read_T(n, dst0, dst1):
                for e, (dst, ready, sem) in enumerate(((dst0, first_done, None), (dst1, slot_done, taken))):
                    dve.wait_ge(ready, n.n(1))
                    tt(dst, ps[:, 2 * n.s + e, :], rstd_row[:, :], ALU.mult, sem)

            def read_V(n, dst, c0):
                for t in range(NT):
                    if t % 2 == 0:
                        dve.wait_ge((first_done, slot_done)[t // 2], n.n(1))
                    ts(dst[:, t, c0:c0 + 256], ps[:, 2 * n.s + t // 2, 256 * (t % 2):256 * (t % 2) + 256],
                       rstd[:, t:t + 1], None, ALU.mult, sem=taken if t == NT - 1 else None)

            def halves(t, size):
                return t[:, :, :].rearrange("p h (n two t) -> p (h n) two t", two=2, t=size)

            def wider(e, size, sem):
                pairs = e[:, :, :].rearrange("p h (n two) -> p (h n) two", two=2)
                n = H * S // (2 * size)
                f, g = halves(hgF, size)[:, :, 0, :], halves(hgQ, size)[:, :, 1, :]
                tt(f, f, pairs[:, :, 1:2].to_broadcast([P, n, size]), ALU.mult)
                tt(g, g, pairs[:, :, 0:1].to_broadcast([P, n, size]), ALU.mult, sem)

            def wide_decay(dst, src):
                v = src[:, :, :].rearrange("p h (n two) -> p h n two", two=2)
                tt(dst[:, :, :], v[:, :, :, 0], v[:, :, :, 1], ALU.mult)

            def level_in(li):
                for i in range(NT):
                    dve.wait_ge(lev_out, 4 * li + i + 1)
                    if li == 3:
                        copy(att[i][0:L, :, L:P], ps[0:L, 4 + i, 0:H * L].rearrange("p (h t) -> p h t", h=H), lev_taken)
                        continue
                    q.sig(dve.copy_predicated(att[i][:, :, 0:P],
                                              masks[:, li, :].bitcast(U32).unsqueeze(1).to_broadcast([P, H, P]),
                                              ps[:, 4 + i, :].rearrange("p (h t) -> p h t", h=H)), lev_taken)

            def row4(t):
                return t.unsqueeze(1).to_broadcast([P, 4, S])

            def job(n):
                if n == 0:
                    dve.wait_ge(row_out, 1)
                    copy(rstd_row[:, :], ps[:, 4, :])
                    q.settle()
                elif n == 1:
                    dve.wait_ge(sin_ready, 2)
                    tt(whole[0][:, :, :], trig[:, 0], trig[:, 0], ALU.mult)
                    q.settle()
                    for b in range(4):
                        ts(wide[:, 0, :, b, :], whole[0][:, :, :], -2.0, 1.0, ALU.mult, ALU.add)
                        ts(wide[:, 1, :, b, :], trig[:, 1], 1.0 if b % 2 else -1.0, None, ALU.mult,
                           sem=wide_ready if b == 3 else None)
                elif n == 2:
                    dve.wait_ge(hg_sig, 1)
                    for h in range(H):
                        ts(hgF[:, h, :], hgF[:, h, :], lb[:, 1, h:h + 1], lb[:, 0, h:h + 1], ALU.mult, ALU.add)
                    q.settle()
                    ts(hgk[:, :, :], hgF[:, :, :], -1.0, 1.0, ALU.mult, ALU.add)
                    ts(hgl[:, :, :], hgF[:, :, :], 2.0 ** 60, 1.0, ALU.mult, ALU.min, hg_arg)
                    q.settle()
                    ts(hgF[:, :, :], hgF[:, :, :], 2.0 ** -60, None, ALU.max, sem=hg_arg)
                    dve.wait_ge(tab_out, 2)
                    copy(cosT[:, :], ps[:, 5, :], tab_ready)
                    copy(sinT[:, :], ps[:, 6, :], tab_ready)
                elif n == 3:
                    dve.wait_ge(hg_ln, 2)
                    tt(hgF[:, :, :], hgF[:, :, :], hgl[:, :, :], ALU.add)
                    q.settle()
                    for h in range(H):
                        q.sig(dve.tensor_tensor_scan(hgG[:, h, :], restart[:, :], hgF[:, h, :], 0.0, ALU.mult,
                                                     ALU.add), hg_G)
                    q.settle()
                    g4 = hgG[:, :, :].rearrange("p h (n t) -> p (h n) t", t=HG_T)
                    tt(hgF[:, :, :].rearrange("p h (n t) -> p (h n) t", t=HG_T),
                       g4[:, :, HG_T - 1:HG_T].to_broadcast([P, H * S // HG_T, HG_T]), g4, ALU.subtract, hg_diff)
                elif n == 4:
                    dve.wait_ge(hg_eG, 1)
                    dve.wait_ge(hg_qs, 1)
                    stt(hgQ[:, :, :], hgQ[:, :, :], float(P) ** -0.5, hgK[:, :, :], ALU.mult, ALU.mult, hg_qin)
                    dve.wait_ge(hg_e16, 1)
                    wide_decay(e32, e16)
                    q.settle()
                    wide_decay(e64, e32)
                    q.settle()
                    wide_decay(e128, e64)
                elif n == 5:
                    dve.wait_ge(hg_enG, 1)
                    tt(hgK[:, :, :], hgK[:, :, :], hgk[:, :, :], ALU.mult, hg_kq)
                    dve.wait_ge(hg_ed, 1)
                    tt(hgF[:, :, :], hgF[:, :, :], hgk[:, :, :], ALU.mult, hg_kq)
                elif n == 6:
                    dve.wait_ge(att_zero, NT)
                    level_in(0)
                elif n == 7:
                    level_in(1)
                    wider(e16, 16, lev_kq)
                elif n == 8:
                    level_in(2)
                    wider(e32, 32, lev_kq)
                elif n == 9:
                    level_in(3)
                    wider(e64, 64, lev_kq)
                elif n == 10:
                    for m, i in enumerate((0, 2)):
                        dve.wait_ge(lev_out, 17 + m)
                        copy(att[i][:, :, P:2 * P], ps[:, 4 + m, :].rearrange("p (h t) -> p h t", h=H), lev_taken)
                    q.settle()
                    f, g = hgF[:, :, 0:P], hgQ[:, :, 3 * P:S]
                    tt(f, f, e128[:, :, 1:2].to_broadcast([P, H, P]), ALU.mult)
                    tt(g, g, e128[:, :, 2:3].to_broadcast([P, H, P]), ALU.mult, lev_kq)
                elif n == 11:
                    for m in range(4):
                        dve.wait_ge(lev_out, 19 + m)
                        i, h0 = m // 2, 2 * (m % 2)
                        copy(att[i][:, h0:h0 + 2, 2 * P - P * i:S - P * i],
                             ps[:, 4 + m, :].rearrange("p (h t) -> p h t", h=2), lev_taken)
                    dve.wait_ge(r_sw, 4)
                    dve.wait_ge(tab_ready, 2)
                    tt(rsw[:, :, :], rsw[:, :, :], row4(sinT[:, :]), ALU.mult)
                elif n == 12:
                    tt(rqk[:, :, :], rqk[:, :, :], row4(cosT[:, :]), ALU.mult)
                    q.settle()
                    tt(rqk[:, :, :], rqk[:, :, :], rsw[:, :, :], ALU.add, r_rope)
                elif n == 13:
                    dve.wait_ge(hg_std, 1)
                    q.sig(dve.reciprocal(statr[:, 0:NT], stat[:, 0:NT]), hg_rs)
                    dve.wait_ge(hg_og, 1)
                    dve.wait_ge(hg_sq, H)
                    for h in range(H):
                        stt(hgY[:, h, :], hgY[:, h, :], par[:, R_HG + h:R_HG + h + 1], hgO[:, h, :], ALU.mult, ALU.mult)
                elif n == 14:
                    dve.wait_ge(hg_row, 1)
                    q.settle()
                    tt(hgY[:, :, :], hgY[:, :, :], row4(ps[:, 4, :]), ALU.mult, hg_yf)
                elif n == 15:
                    dve.wait_ge(hg_hi, 1)
                    tt(ycL[:, :, :], hgY[:, :, :], ycH[:, :, :].bitcast(F32), ALU.subtract, yc_ready)
                    for h in range(H):
                        dve.wait_ge(r_sc, h + 1)
                        tt(att[0][:, h, :], ps[:, 4 + h, :], decay[:, h, :], ALU.mult, r_att)
                elif n == 16:
                    for h in range(H):
                        dve.wait_ge(r_sc, H + h + 1)
                        tt(att[1][:, h, :], ps[:, 4 + h, 0:S - P], decay[:, h, 0:S - P], ALU.mult, r_att)
                elif n == 17:
                    for m, (i, r) in enumerate(((2, 0), (2, 1), (3, 0), (3, 1))):
                        w = S - P * i
                        dve.wait_ge(r_sc, 2 * H + m + 1)
                        tt(att[i][:, :, :].rearrange("p (v r) t -> p r v t", r=2)[:, r],
                           ps[:, 4 + m, :].rearrange("p (v t) -> p v t", v=2)[:, :, 0:w],
                           decay[:, :, 0:w].rearrange("p (v r) t -> p r v t", r=2)[:, r], ALU.mult, r_att)
                    q.settle()
                    n = Slot(N_G0 - 1)
                    dve.wait_ge(slot_done, n.n(1))
                    tt(svT[:, :], ps[:, 2 * n.s + 1, :], rstd_row[:, :], ALU.mult, taken)
                elif n == 18:
                    dve.wait_ge(s_sw, 8)
                    tt(sq[:, :, :], sq[:, :, :], row4(cosT[:, :]), ALU.mult)
                    tt(sk[:, :], sk[:, :], cosT[:, :], ALU.mult)
                    tt(ssw[:, :, :], ssw[:, :, :], row4(sinT[:, :]), ALU.mult)
                    tt(ssk[:, :], ssk[:, :], sinT[:, :], ALU.mult)
                    q.settle()
                    tt(sk[:, :], sk[:, :], ssk[:, :], ALU.add, s_rope)
                    dve.wait_ge(r_o, H)
                    for v in range(2):
                        a, b = (t[:, 2 * v:2 * v + 2, :].rearrange("p a (c t) -> p a c t", t=L) for t in (sq, ssw))
                        tt(sqc[:, v].rearrange("p c a t -> p a c t"), a, b, ALU.add, s_rope)
                elif n == 19:
                    dve.wait_ge(sv_T, 1)
                    copy(sv[:, :, :], ps[:, 5, :].rearrange("p (t c) -> p t c", t=NT), sv_ready)
                    dve.wait_ge(r_std, 1)
                    q.sig(dve.reciprocal(statr[:, :], stat[:, :]), r_rs)
                    dve.wait_ge(r_g, 1)
                    dve.wait_ge(r_sqd, H)
                    tt(rY[:, :, :], rY[:, :, :], rG[:, :, :], ALU.mult)
                elif n == 20:
                    dve.wait_ge(r_row, 4)
                    q.settle()
                    tt(rY[:, :, :], rY[:, :, :], ps[:, 4:8, :], ALU.mult, r_yf)
                elif n == 21:
                    softmax_in(0)
                    dve.wait_ge(r_hi, 1)
                    tt(yaL[:, :, :], rY[:, :, :], yaH[:, :, :].bitcast(F32), ALU.subtract, ya_ready)
                elif n == 22:
                    softmax_out(0)
                    softmax_in(1)
                elif n == 23:
                    softmax_out(1)
                elif n in (24, 26):
                    hf = (n - 24) // 2
                    dve.wait_ge(s_hi, hf + 1)
                    f = slice(256 * hf, 256 * hf + 256)
                    tt(ybL[:, :, f], ps[:, 4:6, :].rearrange("p v (a t) -> p (v a) t", a=2), ybH[:, :, f].bitcast(F32),
                       ALU.subtract, yb_ready)
                elif n == 25:
                    dve.wait_ge(m_std, 1)
                    q.sig(dve.reciprocal(memst[:, 4:6], memst[:, 2:4]), m_rs)

            def softmax_in(hf):
                dve.wait_ge(s_sc, hf + 1)
                scores = ps[:, 4:8, :].rearrange("p b (u t) -> p (b u) t", u=4)
                q.sig(dve.reduce_max(smx[:, hf, :], scores, AX_X))
                q.settle()
                s16 = sink16[:, :, :, :, :].rearrange("p a b c d -> p (a b c d)")
                stt(smx[:, hf, :], smx[:, hf, :], float(L) ** -0.5, s16, ALU.mult, ALU.max)
                q.settle()
                tt(snk[:, hf, :], s16, smx[:, hf, :], ALU.subtract)
                stt(sP[hf][:, :, :], scores, float(L) ** -0.5, smx[:, hf, :].unsqueeze(2).to_broadcast([P, 16, P]),
                    ALU.mult, ALU.subtract, s_arg)

            def softmax_out(hf):
                dve.wait_ge(s_exp, hf + 1)
                if hf == 0:
                    for r in range(2):
                        q.sig(dve.memset(sP[0][:, 4 * r:4 * r + 2, L:2 * L], 0.0))
                    q.settle()
                q.sig(dve.reduce_sum(ssum[:, hf, :], sP[hf][:, :, :], AX_X))
                q.settle()
                tt(ssum[:, hf, :], ssum[:, hf, :], snk[:, hf, :], ALU.add)
                q.settle()
                q.sig(dve.reciprocal(ssum[:, hf, :], ssum[:, hf, :]))
                q.settle()
                tt(sP[hf][:, :, :], sP[hf][:, :, :], ssum[:, hf, :].unsqueeze(2).to_broadcast([P, 16, P]), ALU.mult,
                   s_prob)

            def gate_in(n):
                dve.wait_ge(first_done, n.n(1))
                tt(gate[n.s][:, :], ps[:, 2 * n.s, :], rstd_row[:, :], ALU.mult, g_in)

            def gate_out(n, dst, sem=taken):
                dve.wait_ge(slot_done, n.n(1))
                dve.wait_ge(g_sig, n.n(1 - N_G0))
                tt(dst, gate[n.s][:, :], ps[:, 2 * n.s + 1, :], ALU.mult, sem)

            pairs = {0: (hgF, 0), 1: (hgF, 2), 2: (hgQ, 0), 3: (hgQ, 2), 6: (hgO, 0), 7: (hgO, 2), 8: (rqk, 0),
                     9: (rqk, 2), 12: (rG, 0), 13: (rG, 2), 14: (sq, 0), 15: (sq, 2)}
            for c in range(N_G0):
                n = Slot(c)
                if c == 5:
                    job(c)
                if c:
                    lo(n + 1, 2048 if c + 1 < N_G0 else 12 * P)
                if c != 5:
                    job(c)
                if c in pairs:
                    t, e = pairs[c]
                    read_T(n, t[:, e, :], t[:, e + 1, :])
                elif c in (4, 5):
                    read_V(n, hgV, 256 * (c - 4))
                elif c in (10, 11):
                    read_V(n, rV, 256 * (c - 10))
                else:
                    dve.wait_ge(first_done, n.n(1))
                    tt(sk[:, :], ps[:, 2 * n.s, :], rstd_row[:, :], ALU.mult)
            for c in range(N_G0, N_LINE):
                n = Slot(c)
                if c == 20:
                    job(c)
                lo(n + 1, 12 * P)
                if c != 20:
                    job(c)
                gate_in(n)
                if c < N_G1:
                    gate_out(n, mix[:, c - N_G0, :])
                else:
                    gate_out(n, gmix[:, :])
                    q.settle()
                    tt(mix[:, c - N_G1, :], mix[:, c - N_G1, :], gmix[:, :], ALU.add)
            for k in range(KD):
                dve.wait_ge(m_hi, k + 1)
                if k % 2 == 1:
                    for e in (k - 1, k):
                        stt(memL[:, e, :], ps[:, 4 + e // 2, 256 * (e % 2):256 * (e % 2) + 256],
                            par[:, G_MEMN + e:G_MEMN + e + 1], memH[:, e, :].bitcast(F32), ALU.mult, ALU.subtract,
                            m_ready if e == k else None)
            turns = (N_G2 - N_LINE) // 2
            with dve.Fori(0, turns) as i:
                q.enter(i, [(lo_ready, 2), (g_in, 2), (taken, 2), (dve_step, 2)])
                for k in range(2):
                    n = Slot(N_LINE + k, i, 2)
                    lo(n + 1, 12 * P)
                    gate_in(n)
                    gate_out(n, gmix[:, :])
                    q.settle()
                    t = mix[:, bass.ds(n.n(-N_G1), 1), :]
                    tt(t, t, gmix[:, :], ALU.add)
                q.leave(turns)
            turns = KD // 2
            with dve.Fori(0, turns) as i:
                q.enter(i, [(lo_ready, 2), (g_in, 2), (taken, 2), (mix_sum, 2), (mix_ready, 2)])
                for k in range(2):
                    n = Slot(N_G2 + k, i, 2)
                    lo(n + 1, 2048)
                    gate_in(n)
                    gate_out(n, gmix[:, :])
                    q.settle()
                    j = n.n(-N_G2)
                    t = mix[:, bass.ds(j, 1), :]
                    tt(t, t, gmix[:, :], ALU.add, mix_sum)
                    dve.wait_ge(mix_hi, n.n(1 - N_G2))
                    tt(mixL[:, bass.ds(j, 1), :], t, mixH[:, bass.ds(j, 1), :].bitcast(F32), ALU.subtract, mix_ready)
                q.leave(turns)

            def new_x(n, c, e, gain):
                t = xT[:, e.n(0 if gain == G_MEM else -KD), :]
                dve.wait_ge((first_done, slot_done)[c], n.n(1))
                if gain == G_MEM:
                    copy(t, ps[:, 2 * n.s + c, :], (x_new, taken)[c])
                else:
                    tt(t, t, ps[:, 2 * n.s + c, :], ALU.add, (x_new, taken)[c])

            def x_lower(e, gain):
                j = e.n(0 if gain == G_MEM else -KD)
                dve.wait_ge(x_hi, e.n(1))
                stt(hL[:, j, :], xT[:, j, :], par[:, gain + j:gain + j + 1], hH[:, j, :].bitcast(F32), ALU.mult,
                    ALU.subtract, x_lo)

            def norm_columns(k):
                dve.wait_ge(n_std, k)
                q.sig(dve.reciprocal(rstd[:, 0:NT], rstd[:, NT:2 * NT]), n_rs)

            def norm_row(k):
                dve.wait_ge(n_row, k)
                copy(rstd_row[:, :], ps[:, 5, :], n_ready)
                q.settle()

            for c in range(4):
                n = Slot(N_OUT + c)
                lo(n + 1)
                for e in range(2):
                    new_x(n, e, Slot(2 * c + e), G_MEM)
                    x_lower(Slot(2 * c + e), G_MEM)

            def read_keys(n, h):
                for e in range(2):
                    dve.wait_ge((first_done, slot_done)[e], n.n(1))
                    copy(mkT[:, h + e, :], ps[:, 2 * n.s + e, 0:M], taken if e else None)

            def read_values(n, c0):
                for t in range(MT):
                    dve.wait_ge((first_done, slot_done)[t], n.n(1))
                    copy(mV[:, t, c0:c0 + 256], ps[:, 2 * n.s + t, 0:256], taken if t else None)

            def a_maximum(h):
                dve.wait_ge(a_sc, h + 1)
                q.sig(dve.reduce_max(mstat[:, 0, h, :], ps[:, 4:6, :].rearrange("p b (t m) -> p (b t) m", t=2), AX_X))
                q.settle()
                ts(mstat[:, 1, h, :], mstat[:, 0, h, :], -float(P) ** -0.5, None, ALU.mult, sem=a_max)

            def a_normed(h):
                dve.wait_ge(a_exp, h + 1)
                q.sig(dve.reciprocal(mstat[:, 3, h, :], mstat[:, 2, h, :]))
                q.settle()
                tt(mP[h % 2][:, :, :], mP[h % 2][:, :, :], mstat[:, 3, h, :].unsqueeze(2).to_broadcast([P, NT, M]),
                   ALU.mult, a_prob)

            def a_lower(h):
                dve.wait_ge(a_hi, h + 1)
                tt(moL[:, h, :], ps[:, h ^ 2, :], moH[:, h, :].bitcast(F32), ALU.subtract, a_ready)

            lo(Slot(N_MQ))
            norm_columns(1)
            read_keys(Slot(N_MK), 0)
            lo(Slot(N_MK + 2))
            norm_row(1)
            read_T(Slot(N_MQ), mq[:, 0, :], mq[:, 1, :])
            lo(Slot(N_MQ + 2))
            read_keys(Slot(N_MK + 2), 2)
            a_maximum(0)
            lo(Slot(N_MV))
            a_normed(0)
            a_maximum(1)
            a_normed(1)
            read_T(Slot(N_MQ + 2), mq[:, 2, :], mq[:, 3, :])
            lo(Slot(N_MV + 1))
            read_values(Slot(N_MV), 0)
            a_maximum(2)
            lo(Slot(N_MO), 4 * 256)
            a_normed(2)
            read_values(Slot(N_MV + 1), 256)
            a_maximum(3)
            lo(Slot(N_MO + 1), 4 * 256)
            a_normed(3)
            for h in range(H):
                a_lower(h)
            for c in range(4):
                n = Slot(N_MO + c)
                e = Slot(KD + 2 * c)
                new_x(n, 0, e, G_FFN)
                if c:
                    x_lower(e + -1, G_FFN)
                new_x(n, 1, e + 1, G_FFN)
                x_lower(e, G_FFN)
                if c == 3:
                    x_lower(e + 1, G_FFN)
                lo(n + 2, 4 * 256 if c < 2 else 2048)

            def up_read(n, e):
                z = (za, zu)[e]
                dve.wait_ge((first_done, slot_done)[e], n.n(1))
                tt(z[:, 2:S + 2], ps[:, 2 * n.s + e, :], rstd_row[:, :], ALU.mult, taken if e else f_z)

            def conv(n, e):
                z, c = ((za, ca), (zu, cu))[e]

                def tap(j):
                    return par[:, bass.ds(n.n(R_CONV + 2 * KF * j + KF * e - N_UP), 1)]

                dve.wait_ge(f_tap[e], n.n(1 - N_UP))
                stt(c[:, :], z[:, 1:S + 1], tap(1), c[:, :], ALU.mult, ALU.add)
                q.settle()
                stt(c[:, :], z[:, 0:S], tap(0), c[:, :], ALU.mult, ALU.add, f_conv if e == 0 else None)

            def ffn(n, lower=True):
                up_read(n, 0)
                if lower:
                    ffn_lower(n + -1)
                conv(n, 0)
                up_read(n, 1)
                conv(n, 1)
                dve.wait_ge(f_silu, n.n(1 - N_UP))
                q.settle()
                tt(prod[:, :], ca[:, :], cu[:, :], ALU.mult, f_prod)
                lo(n + 2)

            def ffn_lower(n):
                dve.wait_ge(f_hi, n.n(1 - N_UP))
                j = bass.ds(n.n(-N_UP), 1)
                tt(actL[:, j, :], prod[:, :], actH[:, j, :].bitcast(F32), ALU.subtract, f_ready)

            q.sig(dve.memset(za[:, 0:2], 0.0))
            q.sig(dve.memset(zu[:, 0:2], 0.0))
            norm_columns(2)
            norm_row(2)
            ffn(Slot(N_UP), lower=False)
            ffn(Slot(N_UP + 1))
            turns = KF // 2 - 1
            with dve.Fori(0, turns) as i:
                q.enter(i, [(lo_ready, 2), (taken, 2), (f_z, 2), (f_conv, 2), (f_prod, 2), (f_ready, 2), (dve_step, 6)])
                for k in range(2):
                    ffn(Slot(N_UP + 2 + k, i, 2))
                q.leave(turns)

            def down_tile(m, qq):
                n = Slot(N_DN + 2 * m.c, m.i, 2 * m.per)
                if m.c < KD - 1:
                    lo(n + 2, KH * P)
                    lo(n + 3, KH * P)
                j = m.n()
                t = xT[:, bass.ds(j, 1), :]
                dve.wait_ge(slot_done, n.n(2))
                tt(t, t, ps[:, 4 + qq, :], ALU.add, o_new)
                if m.c:
                    dve.wait_ge(o_T, m.n())
                q.settle()
                ts(xg[:, :], t, par[:, bass.ds(m.n(G_FIN), 1)], None, ALU.mult, sem=o_g)
                if m.c == KD - 1:
                    return
                dve.wait_ge(o_sq, m.n(1))
                tt(ssqF[:, :], ssqF[:, :], fsq[:, :], ALU.add, o_acc)

            ffn_lower(Slot(N_DN - 1))
            q.sig(dve.memset(ssqF[:, :], 0.0))
            q.settle()
            down_tile(Slot(0), 0)
            down_tile(Slot(1), 1)
            turns = KD // 2 - 2
            with dve.Fori(0, turns) as i:
                q.enter(i, [(lo_ready, 4), (o_new, 2), (o_g, 2), (o_acc, 2)])
                for k in range(2):
                    down_tile(Slot(2 + k, i, 2), k)
                q.leave(turns)
            down_tile(Slot(KD - 2), 0)
            down_tile(Slot(KD - 1), 1)
            dve.wait_ge(o_std, 1)
            q.sig(dve.reciprocal(rstd[:, 0:NT], rstd[:, NT:2 * NT]))
            q.settle()
            dve.wait_ge(o_tok, KD)
            for t in range(NT):
                ts(otok[:, t, :], otok[:, t, :], rstd[:, t:t + 1], None, ALU.mult, sem=o_fin)


_INS = ["x", "mem", "positions", "norm_mix_g", "w_in", "swa_sinks", "hg_lb_logits", "hg_norm_g", "w_branch", "w_out",
        "norm_mem_g", "mem_norm_g", "w_mq", "w_mkv", "w_mo", "norm_ffn_g", "w_up", "conv_w", "conv_b", "w_down",
        "final_norm_g"]


def shape_constants():
    c = np.zeros((P, K_ALL), np.float32)
    c[:, K_ID:K_ID + P] = np.eye(P)
    s, t = np.arange(P)[:, None], np.arange(P)[None, :]
    c[:, K_MASK:K_MASK + P] = (s // HG_T == t // HG_T) & (t >= s)
    for i, size in enumerate((16, 32, 64)):
        c[:, K_MASK + P * (i + 1):K_MASK + P * (i + 2)] = (s // size % 2 == 0) & (t // size == s // size + 1)
    j, p = np.arange(S)[None, :], np.arange(P)[:, None]
    for h in range(H):
        log_gamma = np.log1p(-(2.0 ** (-5 - h)))
        c[:, K_DECAY + S * h:K_DECAY + S * (h + 1)] = np.where(j >= p, np.exp(log_gamma * np.maximum(j - p, 0)), 0) / 8
    f = np.float32
    c[:, K_INV:K_INV + 32] = f(1.0) / (f(10000.0) ** (np.arange(0, 64, 2, dtype=f) / f(64)))
    return c


def kernel(**inputs):
    import concourse.bacc as _bacc
    from concourse.bass_utils import run_bass_kernel_spmd as _run

    nc = _bacc.Bacc("TRN2", target_bir_lowering=False, num_devices=1)
    arrays, args = {}, []
    for name, a in [(name, inputs[name]) for name in _INS] + [("consts", shape_constants())]:
        a = np.ascontiguousarray(a)
        arrays[f"in_{name}"] = a
        args.append(nc.dram_tensor(f"in_{name}", a.shape, mybir.dt.from_np(a.dtype), kind="ExternalInput").ap())
    args.append(nc.dram_tensor("out", (1, S, D), F32, kind="ExternalOutput").ap())
    hybrid_layer(nc, *args)
    r = _run(nc, [arrays], core_ids=[0])
    return r.results[0]["out"]
```
